# Optimizing a Trainium2 kernel written in Bass

```python
import jax, jax.numpy as jnp
from jax import lax
import numpy as np

D_MODEL = 2048
BATCH = 1
SEQ = 256
DEPTH = 2

EPS = 1e-6
N_EVEN = (DEPTH + 1) // 2
N_ODD = DEPTH // 2
D_A = D_MODEL // 2
POOL_WINDOWS = (2, 4, 8, 16)
N_POOL_GROUPS = len(POOL_WINDOWS)
G_A = D_A // N_POOL_GROUPS
D_B = D_MODEL // 2
H_B = 4
DH_B = D_B // H_B
CHUNK = 128
D_IN_AB = D_A + 2 * D_B
D_MIX_AB = D_A + D_B
D_C = D_MODEL
CONV_K = 31
D_FF = ((8 * D_MODEL // 3 + 255) // 256) * 256

kernel_name = "hybrid_pool_sgu_conformer_block"

def rms_norm(x, g):
    xf = x.astype(jnp.float32)
    y = xf * lax.rsqrt(jnp.mean(xf * xf, axis=-1, keepdims=True) + EPS)
    return (y * g.astype(jnp.float32)).astype(x.dtype)

def layer_norm(x, g, b):
    xf = x.astype(jnp.float32)
    mu = jnp.mean(xf, axis=-1, keepdims=True)
    var = jnp.mean(jnp.square(xf - mu), axis=-1, keepdims=True)
    y = (xf - mu) * lax.rsqrt(var + EPS)
    return (y * g.astype(jnp.float32) + b.astype(jnp.float32)).astype(x.dtype)

def causal_window_mean(x, w):
    s = x.shape[1]
    cs = jnp.cumsum(x.astype(jnp.float32), axis=1)
    lag = jnp.pad(cs, ((0, 0), (w, 0), (0, 0)))[:, :s]
    count = jnp.minimum(jnp.arange(s) + 1, w).astype(jnp.float32)
    return ((cs - lag) / count[None, :, None]).astype(x.dtype)

def pool_mixer(a, w_group, scale):
    outs = []
    for g, w in enumerate(POOL_WINDOWS):
        ag = a[..., g * G_A:(g + 1) * G_A]
        d = causal_window_mean(ag, w) - ag
        outs.append(jnp.einsum('bsc,cd->bsd', d, w_group[g]))
    return jnp.concatenate(outs, axis=-1) * scale

def sgu_mixer(z, ln_g, ln_b, w_s, b_s):
    u, v = z[..., :D_B], z[..., D_B:]
    v = layer_norm(v, ln_g, ln_b)
    bsz, s, _ = v.shape
    v = v.reshape(bsz, s // CHUNK, CHUNK, H_B, DH_B)
    mask = jnp.tril(jnp.ones((CHUNK, CHUNK), dtype=bool))
    w = jnp.where(mask[None], w_s, jnp.zeros_like(w_s))
    mixed = jnp.einsum('hts,bcshd->bcthd', w, v) + b_s.T[None, None, :, :, None]
    return u * mixed.reshape(bsz, s, D_B)

def ab_layer(x, norm_pre, w_in, a_w_group, a_scale, b_ln_g, b_ln_b, b_w_s, b_b_s,
             w_out, norm_post):
    h = rms_norm(x, norm_pre)
    p = jnp.einsum('bsd,de->bse', h, w_in)
    a_out = pool_mixer(p[..., :D_A], a_w_group, a_scale)
    b_out = sgu_mixer(jax.nn.gelu(p[..., D_A:]), b_ln_g, b_ln_b, b_w_s, b_b_s)
    y = jnp.einsum('bse,ed->bsd', jnp.concatenate([a_out, b_out], axis=-1), w_out)
    return x + rms_norm(y, norm_post)

def conformer_conv_layer(x, norm_pre, w_pw1, b_pw1, w_dw, b_dw, ln_g, ln_b,
                         w_pw2, b_pw2, norm_post):
    h = rms_norm(x, norm_pre)
    p = jnp.einsum('bsd,de->bse', h, w_pw1) + b_pw1
    g = p[..., :D_C] * jax.nn.sigmoid(p[..., D_C:])
    conv = lax.conv_general_dilated(
        g, w_dw[:, None, :], window_strides=(1,), padding=[(CONV_K - 1, 0)],
        dimension_numbers=('NWC', 'WIO', 'NWC'), feature_group_count=D_C) + b_dw
    c = jax.nn.silu(layer_norm(conv, ln_g, ln_b))
    y = jnp.einsum('bse,ed->bsd', c, w_pw2) + b_pw2
    return x + rms_norm(y, norm_post)

def swiglu_ffn(x, norm_pre, w_gate, w_up, w_down, norm_post):
    h = rms_norm(x, norm_pre)
    a = jax.nn.silu(jnp.einsum('bsd,df->bsf', h, w_gate)) * jnp.einsum('bsd,df->bsf', h, w_up)
    y = jnp.einsum('bsf,fd->bsd', a, w_down)
    return x + rms_norm(y, norm_post)

def setup_inputs(seed: int = 0) -> dict:
    key = jax.random.key(seed)
    ks = jax.random.split(key, 32)
    f32 = jnp.float32
    nrm = lambda k, shape, scale: (jax.random.normal(k, shape, f32) * scale).astype(f32)
    gain = lambda k, shape: 1.0 + 0.05 * jax.random.normal(k, shape, f32)
    bias = lambda k, shape: 0.02 * jax.random.normal(k, shape, f32)
    NE, NO, L = N_EVEN, N_ODD, DEPTH
    return {
        "x": jax.random.normal(ks[0], (BATCH, SEQ, D_MODEL), f32),
        "ab_norm_pre": gain(ks[1], (NE, D_MODEL)),
        "ab_w_in": nrm(ks[2], (NE, D_MODEL, D_IN_AB), D_MODEL ** -0.5),
        "a_w_group": nrm(ks[3], (NE, N_POOL_GROUPS, G_A, G_A), G_A ** -0.5),
        "a_scale": 0.5 + 0.1 * jax.random.normal(ks[4], (NE, D_A), f32),
        "b_ln_g": gain(ks[5], (NE, D_B)),
        "b_ln_b": bias(ks[6], (NE, D_B)),
        "b_w_s": nrm(ks[7], (NE, H_B, CHUNK, CHUNK), CHUNK ** -0.5),
        "b_b_s": gain(ks[8], (NE, H_B, CHUNK)),
        "ab_w_out": nrm(ks[9], (NE, D_MIX_AB, D_MODEL), D_MIX_AB ** -0.5),
        "ab_norm_post": gain(ks[10], (NE, D_MODEL)),
        "c_norm_pre": gain(ks[11], (NO, D_MODEL)),
        "c_w_pw1": nrm(ks[12], (NO, D_MODEL, 2 * D_C), D_MODEL ** -0.5),
        "c_b_pw1": bias(ks[13], (NO, 2 * D_C)),
        "c_w_dw": nrm(ks[14], (NO, CONV_K, D_C), CONV_K ** -0.5),
        "c_b_dw": bias(ks[15], (NO, D_C)),
        "c_ln_g": gain(ks[16], (NO, D_C)),
        "c_ln_b": bias(ks[17], (NO, D_C)),
        "c_w_pw2": nrm(ks[18], (NO, D_C, D_MODEL), D_C ** -0.5),
        "c_b_pw2": bias(ks[19], (NO, D_MODEL)),
        "c_norm_post": gain(ks[20], (NO, D_MODEL)),
        "f_norm_pre": gain(ks[21], (L, D_MODEL)),
        "f_w_gate": nrm(ks[22], (L, D_MODEL, D_FF), D_MODEL ** -0.5),
        "f_w_up": nrm(ks[23], (L, D_MODEL, D_FF), D_MODEL ** -0.5),
        "f_w_down": nrm(ks[24], (L, D_FF, D_MODEL), D_FF ** -0.5),
        "f_norm_post": gain(ks[25], (L, D_MODEL)),
    }

def reference(x, ab_norm_pre, ab_w_in, a_w_group, a_scale, b_ln_g, b_ln_b, b_w_s, b_b_s,
              ab_w_out, ab_norm_post, c_norm_pre, c_w_pw1, c_b_pw1, c_w_dw, c_b_dw,
              c_ln_g, c_ln_b, c_w_pw2, c_b_pw2, c_norm_post, f_norm_pre, f_w_gate,
              f_w_up, f_w_down, f_norm_post):
    for layer in range(DEPTH):
        i = layer // 2
        if layer % 2 == 0:
            x = ab_layer(x, ab_norm_pre[i], ab_w_in[i], a_w_group[i], a_scale[i],
                         b_ln_g[i], b_ln_b[i], b_w_s[i], b_b_s[i], ab_w_out[i],
                         ab_norm_post[i])
        else:
            x = conformer_conv_layer(x, c_norm_pre[i], c_w_pw1[i], c_b_pw1[i], c_w_dw[i],
                                     c_b_dw[i], c_ln_g[i], c_ln_b[i], c_w_pw2[i],
                                     c_b_pw2[i], c_norm_post[i])
        x = swiglu_ffn(x, f_norm_pre[layer], f_w_gate[layer], f_w_up[layer],
                       f_w_down[layer], f_norm_post[layer])
    return x


_drawn_inputs = setup_inputs


def setup_inputs(seed=0):
    import zlib

    import numpy as np

    out = dict(_drawn_inputs(seed))
    spreads = {}
    factors = {'b_ln_b': 5.994, 'c_b_pw1': 4.765, 'c_ln_b': 5.033, 'c_b_pw2': 3.196}
    for name, (base, spread) in spreads.items():
        noise = np.random.default_rng([zlib.crc32(name.encode()), seed]).standard_normal(out[name].shape)
        drawn = base * np.exp(spread * noise) if base else spread * noise
        out[name] = __import__('jax').numpy.asarray(drawn.astype(out[name].dtype))
    for name, factor in factors.items():
        out[name] = (out[name] * factor).astype(out[name].dtype)
    return out
```

```python
from contextlib import ExitStack

import concourse.bass as bass
import numpy as np
from concourse import mybir

F32 = mybir.dt.float32
F32R = mybir.dt.float32r
ALU = mybir.AluOpType
ACT = mybir.ActivationFunctionType
AX = mybir.AxisListType

P = 128
D = 2048
SEQ = 256
T = SEQ // P
KT = D // P
DA = D // 2
DFF = 5632
FT = DFF // P
WINDOWS = (2, 4, 8, 16)
HEADS = 4
TAPS = 31
PAD = TAPS - 1
EPS = 1e-6
UNIT = 1024
BANK = 512
FFC = DFF // BANK
CC = 256
CCH = D // CC

Q_V = 0
Q_CONST = 4
Q_A = 5
Q_U = 9
Q_OUT = 13
Q_F0 = Q_OUT + 8
Q_FF = FFC * KT // 4
Q_DOWN = 2 * FT // 4
Q_PW1 = Q_F0 + Q_FF + Q_DOWN
Q_PW2 = Q_PW1 + CCH * KT // 2 // 4
Q_F1 = Q_PW2 + 8
Q_END = Q_F1 + Q_FF + Q_DOWN
Y_LAST = [(Q_OUT + 3, Q_OUT + 7), (Q_F0 + Q_FF + FFC - 1, Q_PW1 - 1), (Q_PW2 + 3, Q_F1 - 1), (Q_F1 + Q_FF + FFC - 1, Q_END - 1)]
SQ_ORDER = [0, 1, 2, 3, 4, 5, CCH - 1, CCH - 2]
Q_POOL0, Q_POOL1 = Q_PW1 + 1, Q_PW2

V_PRE = {"ab": 0, "f0": 16, "c": 32, "f1": 48}
V_ASCALE = 64
V_BA, V_BG, V_BDW, V_LNG, V_LNB = 72, 88, 104, 120, 136
V_ALL = 152


def hi_count(q, s):
    return q * 4 + (s + 1)


def used_count(q, s):
    before_consts = isinstance(q, int) and q < Q_CONST
    return (q if before_consts else q - 1) * 4 + (s + 1)


def lo_count(q, s, after_pool=False):
    return (q - (Q_POOL1 - Q_POOL0 if after_pool else 0)) * 4 + (s + 1)


def y_square(e, t, c):
    at = 2 * t + c if c < 2 else 2 + c + t * (6 if e == 1 else 2)
    return 8 + 16 * e + at


def x_square(b, t, c):
    if b == 0:
        return 4 * t + c
    return 8 + 16 * (b - 1) + (6 * (t + 1) + c if b == 2 else 8 + 4 * t + c)


def x_place(b, t, c):
    return 8 * b + (4 * t + c if b % 2 == 0 else 4 * (c // 2) + 2 * t + c % 2)


def lo_pool_count(q, s):
    return (q - Q_POOL0) * 4 + (s + 1)


def trunk(nc, d_x, d_units, d_vecs, d_taps, d_ident, d_bs, d_lng, d_lnb, d_bpw2, d_post, d_out):
    with ExitStack() as ctx:
        sb = lambda name, shape, dt=F32: ctx.enter_context(nc.sbuf_tensor(name, shape, dt))
        sem = lambda name: ctx.enter_context(nc.semaphore(name))

        x = sb("x", [P, T, D])
        xT_hi = sb("xT_hi", [P, KT, SEQ], F32R)
        xT_lo = sb("xT_lo", [P, KT, SEQ], F32R)
        raw = sb("raw", [P, 4, UNIT])
        w_hi = sb("w_hi", [P, 4, UNIT], F32R)
        w_lo = sb("w_lo", [P, 4, UNIT], F32R)
        gpost = sb("gpost", [P, D])
        tok = sb("tok", [P, D])
        junk = sb("junk", [P, 2, BANK])
        vecs = sb("vecs", [P, V_ALL])
        ident = sb("ident", [P, P])
        warm = sb("warm", [P, 1])
        pow_exp = sb("pow_exp", [P, 1])
        y_sums = sb("y_sums", [P, T, 4])
        x_sums = sb("x_sums", [P, T, 4])
        y_var = sb("y_var", [P, T, 2])
        x_var = sb("x_var", [P, T, 2])
        y_rs = sb("y_rs", [P, T])
        x_rs = sb("x_rs", [P, T])
        acc = ctx.enter_context(nc.psum_tensor("acc", [P, 8, BANK], F32))

        with ExitStack() as m:
            mb = lambda name, shape, dt=F32: m.enter_context(nc.sbuf_tensor(name, shape, dt))
            mix_hi = mb("mix_hi", [P, KT, SEQ], F32R)
            mix_lo = mb("mix_lo", [P, KT, SEQ], F32R)
            vm = mb("vm", [P, D])
            vd_hi = mb("vd_hi", [P, D], F32R)
            vd_lo = mb("vd_lo", [P, D], F32R)
            c_hi = mb("c_hi", [P, 4, UNIT], F32R)
            c_lo = mb("c_lo", [P, 4, UNIT], F32R)
            bs = mb("bs", [P, HEADS, P])
            bn = mb("bn", [P, T, 12])
            mv = mb("mv", [P, T, 2])
            ln_var = mb("ln_var", [P, T])
            ln_rs = mb("ln_rs", [P, T])
        with ExitStack() as m:
            mb = lambda name, shape, dt=F32: m.enter_context(nc.sbuf_tensor(name, shape, dt))
            cT_hi = mb("cT_hi", [P, KT, SEQ], F32R)
            cT_lo = mb("cT_lo", [P, KT, SEQ], F32R)
            conv = mb("conv", [P, KT, SEQ])
            taps = mb("taps", [P, KT, TAPS])
            taps_now = mb("taps_now", [P, 2, TAPS])
            g_now = mb("g_now", [P, 2, PAD + SEQ])
            g_last = mb("g_last", [P, 2, PAD + SEQ])
            sig = mb("sig", [P, 2, 2, SEQ])
            lin = mb("lin", [P, 2, 2, SEQ])
            sq = mb("sq", [P, 2, 2, SEQ])
            prod = mb("prod", [P, 4, SEQ])
            one_mean = mb("one_mean", [P, 1])
            ones = mb("ones", [P, P])
            cst = mb("cst", [P, T, 2])
            cvar = mb("cvar", [P, T, 2])
            crs = mb("crs", [P, T])
            diag = mb("diag", [P, 2, SEQ])
        with ExitStack() as m:
            mb = lambda name, shape, dt=F32: m.enter_context(nc.sbuf_tensor(name, shape, dt))
            hT_hi = mb("hT_hi", [P, FT, SEQ], F32R)
            hT_lo = mb("hT_lo", [P, FT, SEQ], F32R)

        raw_landed = [sem(f"raw_landed{s}") for s in range(4)]
        x_landed = [[sem(f"x_landed{t}{h}") for h in range(2)] for t in range(T)]
        vecs_landed = sem("vecs_landed")
        ident_landed = sem("ident_landed")
        post_landed = sem("post_landed")
        bs_landed = sem("bs_landed")
        lngb_landed = sem("lngb_landed")
        taps_landed = sem("taps_landed")
        bpw2_landed = sem("bpw2_landed")
        out_stored = sem("out_stored")
        hi_ready = sem("hi_ready")
        lo_ready = sem("lo_ready")
        lo_ready_pool = sem("lo_ready_pool")
        units_used = sem("units_used")
        consts_set = sem("consts_set")
        w_s_masked = sem("w_s_masked")
        y0_ready = sem("y0_ready")
        squared = sem("squared")
        y_gained = sem("y_gained")
        y_var_ready = sem("y_var_ready")
        y_rs_ready = sem("y_rs_ready")
        x_ready = sem("x_ready")
        x_var_ready = sem("x_var_ready")
        x_rs_ready = sem("x_rs_ready")
        xn_ready = sem("xn_ready")
        xn_turned = sem("xn_turned")
        xT_hi_ready = sem("xT_hi_ready")
        xT_lo_ready = sem("xT_lo_ready")
        dve_step = sem("dve_step")
        in0_ready = sem("in0_ready")
        v_gelu = sem("v_gelu")
        v_var_ready = sem("v_var_ready")
        v_rs_ready = sem("v_rs_ready")
        v_normed = sem("v_normed")
        v_hi_ready = sem("v_hi_ready")
        v_lo_ready = sem("v_lo_ready")
        mixed_ready = sem("mixed_ready")
        mixed_kept = sem("mixed_kept")
        a_hi_ready = sem("a_hi_ready")
        a_lo_ready = sem("a_lo_ready")
        pooled_ready = sem("pooled_ready")
        pd_hi_ready = sem("pd_hi_ready")
        pd_lo_ready = sem("pd_lo_ready")
        group_ready = sem("group_ready")
        ga_hi_ready = sem("ga_hi_ready")
        ga_lo_ready = sem("ga_lo_ready")
        u_gelu = sem("u_gelu")
        gated_ready = sem("gated_ready")
        gb_hi_ready = sem("gb_hi_ready")
        gb_lo_ready = sem("gb_lo_ready")
        gu0_ready = sem("gu0_ready")
        silu_ready = sem("silu_ready")
        hid_ready = sem("hid_ready")
        hid_turned = sem("hid_turned")
        hT_hi_ready = sem("hT_hi_ready")
        hT_lo_ready = sem("hT_lo_ready")
        glu_ready = sem("glu_ready")
        tap_done = sem("tap_done")
        taps_copied = sem("taps_copied")
        conv_ready = sem("conv_ready")
        gate_ready = sem("gate_ready")
        conv_last_ready = sem("conv_last_ready")
        prod_ready = sem("prod_ready")
        prod_used = sem("prod_used")
        cst_diag_ready = sem("cst_diag_ready")
        cst_spread = sem("cst_spread")
        sq_ready = sem("sq_ready")
        sq_used = sem("sq_used")
        cvar_ready = sem("cvar_ready")
        crs_ready = sem("crs_ready")
        c_normed = sem("c_normed")
        c_silu = sem("c_silu")
        cT_hi_ready = sem("cT_hi_ready")
        cT_lo_ready = sem("cT_lo_ready")

        def y_bank(par, t, c):
            return 4 * (par if c >= 2 else 1 - par) + 2 * t + c % 2

        def wait_sum(eng, t, ready0, count0, q):
            if t == 0:
                eng.wait_ge(ready0, count0)
            else:
                eng.wait_ge(units_used, used_count(q, 3))

        def wait_y(eng, e, j, t):
            wait_sum(eng, t, y0_ready, 2 * e + j + 1, Y_LAST[e][j])

        def pairs(bank):
            return acc[:, bank, :].rearrange("p (k n) -> p k n", n=P)

        block = ctx.enter_context(nc.Block())

        @block.sync
        def _(sp):
            for t in range(T):
                for h in range(2):
                    hs = slice(h * UNIT, (h + 1) * UNIT)
                    sp.dma_start(x[:, t, hs], d_x[t * P:(t + 1) * P, hs]).then_inc(x_landed[t][h], 16)
                if t == 0:
                    sp.dma_start(vecs[:], d_vecs).then_inc(vecs_landed, 16)
                    sp.dma_start(ident[:], d_ident).then_inc(ident_landed, 16)

            def load(q, s):
                sp.dma_start(raw[:, s, :], d_units[q * 4 + s]).then_inc(raw_landed[s], 16)

            for s in range(4):
                load(0, s)
            with sp.Fori(1, Q_POOL0 + 1) as q:
                for s in range(4):
                    sp.wait_ge(lo_ready, lo_count(q - 1, s))
                    load(q, s)
            with sp.Fori(Q_POOL0 + 1, Q_POOL1 + 1) as q:
                for s in range(4):
                    sp.wait_ge(lo_ready_pool, lo_pool_count(q - 1, s))
                    load(q, s)
            with sp.Fori(Q_POOL1 + 1, Q_END) as q:
                for s in range(4):
                    sp.wait_ge(lo_ready, lo_count(q - 1, s, True))
                    load(q, s)
            for t in range(T):
                for h in range(2):
                    hs = slice(h * UNIT, (h + 1) * UNIT)
                    sp.wait_ge(x_ready, x_place(4, t, 2 * h + 1) - 7)
                    sp.dma_start(d_out[t * P:(t + 1) * P, hs], x[:, t, hs]).then_inc(out_stored, 16)
            sp.wait_ge(out_stored, 32 * T)

        @block.gpsimd
        def _(pool):
            def inv_root(ready, count, out, var, done):
                pool.wait_ge(ready, count)
                nc.gpsimd.tensor_tensor(out, var, pow_exp[:].to_broadcast([P, out.shape[-1]]), ALU.pow).then_inc(done, 1)

            def load_post(e):
                if e:
                    pool.wait_ge(y_gained, 8 * e)
                pool.dma_start(gpost[:], d_post[e:e + 1, :].to_broadcast([P, D])).then_inc(post_landed, 16)

            def norm_in(b):
                for t in range(T):
                    inv_root(x_var_ready, 2 * b + t + 1, x_rs[:, t:t + 1], x_var[:, t, 1:2], x_rs_ready)

            def norm_out(e):
                y = [(y_var_ready, 2 * e + t + 1, y_rs[:, t:t + 1], y_var[:, t, 1:2], y_rs_ready) for t in range(T)]
                x_ = [(x_var_ready, 2 * e + t + 3, x_rs[:, t:t + 1], x_var[:, t, 1:2], x_rs_ready) for t in range(T)]
                for root in (y[0], x_[0], y[1], x_[1]) if e == 1 else y if e == 3 else y + x_:
                    inv_root(*root)

            nc.gpsimd.memset(pow_exp[:], -0.5).then_inc(consts_set, 1)
            pool.wait_ge(consts_set, 1)
            norm_in(0)
            load_post(0)
            pool.dma_start(bs[:], d_bs[0:1].to_broadcast([P, HEADS, P])).then_inc(bs_landed, 16)
            pool.wait_ge(xn_turned, 8)
            pool.dma_start(tok[:, 0:DA], d_lng[0:1, :].to_broadcast([P, DA])).then_inc(lngb_landed, 16)
            pool.dma_start(tok[:, DA:D], d_lnb[0:1, :].to_broadcast([P, DA])).then_inc(lngb_landed, 16)
            pool.wait_ge(raw_landed[3], 16 * (Q_CONST + 1))
            w_s = raw[:, 3, BANK:].rearrange("p (h n) -> p h n", h=HEADS)
            nc.gpsimd.affine_select(out=w_s, in_=w_s, compare_op=ALU.is_ge, fill=0.0, base=0,
                                    pattern=[[0, HEADS], [1, P]], channel_multiplier=-1).then_inc(w_s_masked, 1)
            for t in range(T):
                inv_root(v_var_ready, t + 1, ln_rs[:, t:t + 1], ln_var[:, t:t + 1], v_rs_ready)
            norm_out(0)
            load_post(1)
            norm_out(1)
            load_post(2)
            wait_y(pool, 1, 1, 1)
            nc.gpsimd.memset(g_now[:, :, 0:PAD], 0.0).then_inc(consts_set, 1)
            nc.gpsimd.memset(g_last[:, :, 0:PAD], 0.0).then_inc(consts_set, 1)
            nc.gpsimd.memset(one_mean[:], 1.0 / D).then_inc(consts_set, 1)
            nc.gpsimd.memset(ones[:], 1.0).then_inc(consts_set, 1)
            pool.dma_start(taps[:], d_taps).then_inc(taps_landed, 16)
            with pool.Fori(Q_POOL0, Q_POOL1) as q:
                for s in range(4):
                    pool.wait_ge(hi_ready, hi_count(q, s))
                    nc.gpsimd.tensor_tensor(w_lo[:, s, :], raw[:, s, :], w_hi[:, s, :],
                                            ALU.subtract).then_inc(lo_ready_pool, 1)
            pool.wait_ge(xn_turned, 24)
            pool.dma_start(tok[0:1, :], d_bpw2[0:1, :]).then_inc(bpw2_landed, 16)
            inv_root(cvar_ready, 1, crs[:], cvar[:, :, 1], crs_ready)
            norm_out(2)
            load_post(3)
            norm_out(3)

        @block.scalar
        def _(act):
            def split(q, s, gain=None, dst=None):
                act.wait_ge(raw_landed[s], (q + 1) * 16)
                if dst is None and not (isinstance(q, int) and q == 0):
                    act.wait_ge(units_used, used_count(q - (2 if isinstance(q, int) and q == Q_A else 1), s))
                out = w_hi[:, s, :] if dst is None else dst[:, s, :]
                scale = 1.0 if gain is None else vecs[:, gain:gain + 1]
                nc.scalar.activation(out, raw[:, s, :], ACT.Copy, scale=scale).then_inc(hi_ready, 1)

            def split_quad(q, gain=None, k0=0):
                for s in range(4):
                    split(q, s, None if gain is None else gain + k0 + s)

            def square(n, src, total):
                if n >= 2:
                    act.wait_ge(squared, n - 1)
                nc.scalar.activation(junk[:, n % 2, :], src, ACT.Square, accum_out=total).then_inc(squared, 1)

            def square_y(e, par, t, cs):
                for c in cs:
                    j = c // 2
                    wait_y(act, e, j, t)
                    square(y_square(e, t, c), acc[:, y_bank(par, t, c), :], y_sums[:, t, c:c + 1])

            def square_x(b, t, cs):
                for c in cs:
                    if b:
                        act.wait_ge(x_ready, x_place(b, t, c) - 7)
                    else:
                        act.wait_ge(x_landed[t][c // 2], 16)
                    square(x_square(b, t, c), x[:, t, c * BANK:(c + 1) * BANK], x_sums[:, t, c:c + 1])

            def scale_x(b, t):
                act.wait_ge(x_rs_ready, 2 * b + t + 1)
                for c in range(4):
                    if t:
                        act.wait_ge(xn_turned, x_place(b, 0, c) + 1)
                    nc.scalar.activation(tok[:, c * BANK:(c + 1) * BANK], x[:, t, c * BANK:(c + 1) * BANK],
                                         ACT.Copy, scale=x_rs[:, t:t + 1]).then_inc(xn_ready, 1)

            def hi_xT(b, par, t, cs, gain=None):
                for c in cs:
                    act.wait_ge(xn_turned, x_place(b, t, c) + 1)
                    src = pairs(y_bank(par, t, c))
                    dst = xT_hi[:, 4 * c:4 * c + 4, t * P:(t + 1) * P]
                    if gain is None:
                        nc.scalar.activation(dst, src, ACT.Copy).then_inc(xT_hi_ready, 1)
                    else:
                        for n in range(4):
                            g = gain + 4 * c + n
                            last = nc.scalar.activation(dst[:, n, :], src[:, n, :], ACT.Copy, scale=vecs[:, g:g + 1])
                        last.then_inc(xT_hi_ready, 1)

            def open_ffn(e, par, q, gain):
                b = e + 1
                square_y(e, par, 0, (2, 3))
                split(q, 0, gain)
                split(q, 1, gain + 1)
                hi_xT(b, par, 0, (0, 1))
                split(q, 2, gain + 2)
                square_y(e, par, 1, (2, 3))
                split(q, 3, gain + 3)
                hi_xT(b, par, 1, (0, 1))
                split_quad(q + 1, gain, 4)
                hi_xT(b, par, 0, (2, 3))
                hi_xT(b, par, 1, (2, 3))
                split_quad(q + 2, gain, 8)
                square_x(b, 0, range(4))
                square_x(b, 1, range(4))
                split_quad(q + 3, gain, 12)

            ab = V_PRE["ab"]
            act.wait_ge(consts_set, 1)
            nc.scalar.activation(warm[:], pow_exp[:], ACT.Square)
            square_x(0, 0, range(4))
            scale_x(0, 0)
            square_x(0, 1, range(4))
            act.wait_ge(vecs_landed, 16)
            hi_xT(0, 1, 0, range(4))
            split(Q_V, 0, ab)
            split(Q_V, 1, ab + 1)
            scale_x(0, 1)
            split(Q_V, 2, ab + 2)
            split(Q_V, 3, ab + 3)
            hi_xT(0, 1, 1, range(4))
            for k in range(1, 4):
                split_quad(Q_V + k, ab, 4 * k)
            for s in range(4):
                if s == 3:
                    act.wait_ge(w_s_masked, 1)
                split(Q_CONST, s, dst=c_hi)
            split_quad(Q_A, ab, 0)
            for t in range(T):
                wait_sum(act, t, in0_ready, 1, Q_V + 3)
                for h in range(2):
                    nc.scalar.activation(vm[:, t * DA + h * BANK:t * DA + (h + 1) * BANK], acc[:, 2 * t + h, :],
                                         ACT.Gelu_apprx_tanh).then_inc(v_gelu, 1)
            split_quad(Q_A + 1, ab, 4)
            for t in range(T):
                act.wait_ge(v_normed, t + 1)
                nc.scalar.activation(vd_hi[:, t * DA:(t + 1) * DA], vm[:, t * DA:(t + 1) * DA],
                                     ACT.Copy).then_inc(v_hi_ready, 1)
            split_quad(Q_A + 2, ab, 8)
            split_quad(Q_A + 3, ab, 12)
            split_quad(Q_U, ab, 0)
            for t in range(T):
                wait_sum(act, t, in0_ready, 2, Q_A + 3)
                for h in range(2):
                    n = t * 4 + h * 2
                    nc.scalar.activation(mix_hi[:, 8 + n:10 + n, :], acc[:, 4 + 2 * t + h, :].rearrange(
                        "p (k n) -> p k n", n=SEQ), ACT.Copy).then_inc(a_hi_ready, 1)
            split_quad(Q_U + 1, ab, 4)
            for g in range(4):
                act.wait_ge(pooled_ready, g + 1)
                nc.scalar.activation(vd_hi[:, g * BANK:(g + 1) * BANK], acc[:, 4 + g, :], ACT.Copy).then_inc(pd_hi_ready, 1)
            split_quad(Q_U + 2, ab, 8)
            for g in range(4):
                act.wait_ge(group_ready, g + 1)
                for n in range(2):
                    k = 2 * g + n
                    last = nc.scalar.activation(mix_hi[:, k, :], acc[:, 4 + g, n * SEQ:(n + 1) * SEQ], ACT.Copy,
                                                scale=vecs[:, V_ASCALE + k:V_ASCALE + k + 1])
                last.then_inc(ga_hi_ready, 1)
            split_quad(Q_U + 3, ab, 12)
            split_quad(Q_OUT)
            for g in range(4):
                act.wait_ge(units_used, used_count(Q_U + 3, 3))
                nc.scalar.activation(acc[:, g, :], acc[:, g, :], ACT.Gelu_apprx_tanh).then_inc(u_gelu, 1)
            for g in range(4):
                act.wait_ge(gated_ready, g + 1)
                nc.scalar.activation(mix_hi[:, 8 + 2 * g:10 + 2 * g, :], vm[:, g * BANK:(g + 1) * BANK].rearrange(
                    "p (k n) -> p k n", n=SEQ), ACT.Copy).then_inc(gb_hi_ready, 1)
            for k in range(1, 4):
                split_quad(Q_OUT + k)
            split_quad(Q_OUT + 4)
            square_y(0, 0, 0, (0, 1))
            square_y(0, 0, 1, (0, 1))
            for k in range(5, 8):
                split_quad(Q_OUT + k)
            open_ffn(0, 0, Q_F0, V_PRE["f0"])

            def ffn(layer, q0, gain, par, e):
                act.wait_ge(x_rs_ready, 2 * (e - 1) + 4)

                def silu(i, bank_par, t):
                    wait_sum(act, t, gu0_ready, i + (11 * layer + 1), i * 4 + (q0 + 3))
                    nc.scalar.activation(tok[:, t * DA + BANK:(t + 1) * DA], acc[:, 4 * bank_par + 2 * t, :],
                                         ACT.Silu, scale=x_rs[:, t:t + 1]).then_inc(silu_ready, 1)

                def hi_hid(i, bank_par, t):
                    act.wait_ge(hid_turned, i * 2 + (22 * layer + t + 1))
                    nc.scalar.activation(hT_hi[:, bass.ts(i, 4), t * P:(t + 1) * P], pairs(4 * bank_par + 2 * t),
                                         ACT.Copy).then_inc(hT_hi_ready, 1)

                def chunk(i, bank_par):
                    split_quad(i * 4 + q0, gain, 0)
                    silu(i - 1, bank_par, 0)
                    silu(i - 1, bank_par, 1)
                    split_quad(i * 4 + (q0 + 1), gain, 4)
                    hi_hid(i - 1, bank_par, 0)
                    hi_hid(i - 1, bank_par, 1)
                    split_quad(i * 4 + (q0 + 2), gain, 8)
                    split_quad(i * 4 + (q0 + 3), gain, 12)

                with act.Fori(0, (FFC - 1) // 2) as n:
                    chunk(n * 2 + 1, par)
                    chunk(n * 2 + 2, 1 - par)
                qd = q0 + Q_FF
                split_quad(qd)
                silu(FFC - 1, par, 0)
                silu(FFC - 1, par, 1)
                split_quad(qd + 1)
                hi_hid(FFC - 1, par, 0)
                hi_hid(FFC - 1, par, 1)
                with act.Fori(qd + 2, qd + Q_DOWN // 2 + 1) as q:
                    split_quad(q)
                square_y(e, par, 0, (0, 1))
                square_y(e, par, 1, (0, 1))
                with act.Fori(qd + Q_DOWN // 2 + 1, qd + Q_DOWN) as q:
                    split_quad(q)

            ffn(0, Q_F0, V_PRE["f0"], 1, 1)
            c_gain = V_PRE["c"]
            square_y(1, 1, 0, (2, 3))
            square_x(2, 0, range(4))
            scale_x(2, 0)
            square_y(1, 1, 1, (2, 3))
            split(Q_PW1, 0)
            hi_xT(2, 1, 0, range(4), c_gain)
            square_x(2, 1, range(4))
            scale_x(2, 1)
            split(Q_PW1, 1)
            hi_xT(2, 1, 1, range(4), c_gain)
            split(Q_PW1, 2)
            split(Q_PW1, 3)

            act.wait_ge(taps_landed, 16)

            def gate(c, par):
                split_quad(c * 2 + (Q_PW1 + 1))
                split_quad(c * 2 + (Q_PW1 + 2))
                act.wait_ge(units_used, used_count(c * 2 + (Q_PW1 + 1), 3))
                if not isinstance(c, int) or c >= 2:
                    act.wait_ge(glu_ready, c * 2 - 2)
                for n in range(2):
                    k = c * 2 + n
                    nc.scalar.activation(sig[:, par, n, :], acc[:, 4 * par + n, SEQ:2 * SEQ], ACT.Sigmoid,
                                         bias=vecs[:, bass.ds(V_BG + k, 1)])
                    last = nc.scalar.activation(lin[:, par, n, :], acc[:, 4 * par + n, 0:SEQ], ACT.Identity,
                                                bias=vecs[:, bass.ds(V_BA + k, 1)])
                last.then_inc(gate_ready, 1)

            gate(0, 0)
            gate(1, 1)
            with act.Fori(1, CCH // 2) as n:
                gate(n * 2, 0)
                gate(n * 2 + 1, 1)

            def square_conv(place, c):
                if c == CCH - 1:
                    act.wait_ge(conv_last_ready, 2)
                else:
                    act.wait_ge(conv_ready, 2 * (c + 1))
                if place >= 2:
                    act.wait_ge(sq_used, place - 1)
                nc.scalar.activation(sq[:, place % 2], conv[:, 2 * c:2 * c + 2, :], ACT.Square).then_inc(sq_ready, 1)

            for place in range(5):
                square_conv(place, SQ_ORDER[place])
            act.wait_ge(glu_ready, 2 * CCH)
            for j in range(TAPS):
                for n in range(2):
                    i = 2 * j + n
                    if i >= 4:
                        act.wait_ge(prod_used, i - 3)
                    k = 2 * (CCH - 1) + n
                    nc.scalar.activation(prod[:, i % 4, :], g_last[:, n, j:j + SEQ], ACT.Copy,
                                         scale=taps[:, k, j:j + 1]).then_inc(prod_ready, 1)
            square_conv(5, SQ_ORDER[5])
            act.wait_ge(prod_used, 2 * TAPS)
            for n in range(2):
                k = 2 * (CCH - 1) + n
                nc.scalar.activation(conv[:, k, :], acc[:, 3, n * SEQ:(n + 1) * SEQ], ACT.Identity,
                                     bias=vecs[:, V_BDW + k:V_BDW + k + 1]).then_inc(conv_last_ready, 1)
            square_conv(6, SQ_ORDER[6])
            square_conv(7, SQ_ORDER[7])
            for c in range(CCH):
                act.wait_ge(c_normed, c + 1)
                for n in range(2):
                    k = 2 * c + n
                    last = nc.scalar.activation(conv[:, k, :], conv[:, k, :], ACT.Silu, bias=vecs[:, V_LNB + k:V_LNB + k + 1],
                                                scale=vecs[:, V_LNG + k:V_LNG + k + 1])
                last.then_inc(c_silu, 1)
                act.wait_ge(c_silu, c + 1)
                nc.scalar.activation(cT_hi[:, 2 * c:2 * c + 2, :], conv[:, 2 * c:2 * c + 2, :],
                                     ACT.Copy).then_inc(cT_hi_ready, 1)
            for k in range(1, 5):
                split_quad(Q_PW2 + k)
            square_y(2, 1, 0, (0, 1))
            square_y(2, 1, 1, (0, 1))
            for k in range(5, 8):
                split_quad(Q_PW2 + k)
            open_ffn(2, 1, Q_F1, V_PRE["f1"])
            ffn(1, Q_F1, V_PRE["f1"], 0, 3)
            square_y(3, 0, 0, (2, 3))
            square_y(3, 0, 1, (2, 3))

        @block.vector
        def _(dve):
            steps = [0]

            def after(ins):
                steps[0] += 1
                ins.then_inc(dve_step, 1)
                dve.wait_ge(dve_step, steps[0])

            def split(q, s, gain=None, dst=None):
                dve.wait_ge(hi_ready, hi_count(q, s))
                out, hi = (w_lo, w_hi) if dst is None else dst
                if gain is None:
                    ins = nc.vector.tensor_tensor(out[:, s, :], raw[:, s, :], hi[:, s, :], ALU.subtract)
                else:
                    ins = nc.vector.scalar_tensor_tensor(out[:, s, :], raw[:, s, :], vecs[:, gain:gain + 1], hi[:, s, :],
                                                         ALU.mult, ALU.subtract)
                ins.then_inc(lo_ready, 1)

            def split_quad(q, gain=None, k0=0):
                for s in range(4):
                    split(q, s, None if gain is None else gain + k0 + s)

            def gain_y(e, par, t, cs):
                dve.wait_ge(post_landed, 16 * (e + 1))
                for c in cs:
                    dve.wait_ge(squared, y_square(e, t, c) + 1)
                    b = y_bank(par, t, c)
                    nc.vector.tensor_tensor(acc[:, b, :], acc[:, b, :], gpost[:, c * BANK:(c + 1) * BANK],
                                            ALU.mult).then_inc(y_gained, 1)

            def mean_square(sums, var, t, count, ready):
                dve.wait_ge(squared, count)
                after(nc.vector.reduce_sum(var[:, t, 0:1], sums[:, t, :], axis=AX.X))
                nc.vector.tensor_scalar(var[:, t, 1:2], var[:, t, 0:1], 1.0 / D, EPS, ALU.mult, ALU.add).then_inc(ready, 1)

            def add_y(e, par, t, cs):
                for c in cs:
                    dve.wait_ge(y_rs_ready, 2 * e + t + 1)
                    dve.wait_ge(y_gained, 8 * e + (2 * t + c if c < 2 else 2 + 2 * t + c) + 1)
                    xs = x[:, t, c * BANK:(c + 1) * BANK]
                    nc.vector.scalar_tensor_tensor(xs, acc[:, y_bank(par, t, c), :], y_rs[:, t:t + 1], xs,
                                                   ALU.mult, ALU.add).then_inc(x_ready, 1)

            def lo_xT(b, par, t, cs, gain=None):
                for c in cs:
                    dve.wait_ge(xT_hi_ready, x_place(b, t, c) + 1)
                    src = pairs(y_bank(par, t, c))
                    hi = xT_hi[:, 4 * c:4 * c + 4, t * P:(t + 1) * P]
                    dst = xT_lo[:, 4 * c:4 * c + 4, t * P:(t + 1) * P]
                    if gain is None:
                        nc.vector.tensor_tensor(dst, src, hi, ALU.subtract).then_inc(xT_lo_ready, 1)
                    else:
                        for n in range(4):
                            g = gain + 4 * c + n
                            last = nc.vector.scalar_tensor_tensor(dst[:, n, :], src[:, n, :], vecs[:, g:g + 1], hi[:, n, :],
                                                                  ALU.mult, ALU.subtract)
                        last.then_inc(xT_lo_ready, 1)

            def open_ffn(e, par, q, gain):
                b = e + 1
                mean_square(y_sums, y_var, 0, y_square(e, 0, 3) + 1, y_var_ready)
                add_y(e, par, 0, (0,))
                split(q, 0, gain)
                add_y(e, par, 0, (1,))
                lo_xT(b, par, 0, (0, 1))
                split(q, 1, gain + 1)
                mean_square(y_sums, y_var, 1, y_square(e, 1, 3) + 1, y_var_ready)
                split(q, 2, gain + 2)
                add_y(e, par, 1, (0, 1))
                split(q, 3, gain + 3)
                lo_xT(b, par, 1, (0, 1))
                gain_y(e, par, 0, (2, 3))
                split(q + 1, 0, gain + 4)
                add_y(e, par, 0, (2, 3))
                split(q + 1, 1, gain + 5)
                gain_y(e, par, 1, (2, 3))
                split(q + 1, 2, gain + 6)
                add_y(e, par, 1, (2, 3))
                split(q + 1, 3, gain + 7)
                lo_xT(b, par, 0, (2, 3))
                split(q + 2, 0, gain + 8)
                lo_xT(b, par, 1, (2, 3))
                for s in range(1, 4):
                    split(q + 2, s, gain + 8 + s)
                for t in range(T):
                    mean_square(x_sums, x_var, t, x_square(b, t, 3) + 1, x_var_ready)
                split_quad(q + 3, gain, 12)

            mean_square(x_sums, x_var, 0, x_square(0, 0, 3) + 1, x_var_ready)
            mean_square(x_sums, x_var, 1, x_square(0, 1, 3) + 1, x_var_ready)
            dve.wait_ge(vecs_landed, 16)
            lo_xT(0, 1, 0, range(4))
            ab = V_PRE["ab"]
            for s in range(4):
                split(Q_V, s, ab + s)
            lo_xT(0, 1, 1, range(4))
            for k in range(1, 4):
                split_quad(Q_V + k, ab, 4 * k)
            for s in range(4):
                split(Q_CONST, s, dst=(c_lo, c_hi))
            split_quad(Q_A, ab, 0)
            for t in range(T):
                for h in range(2):
                    dve.wait_ge(v_gelu, 2 * t + h + 1)
                    last = nc.vector.bn_stats(bn[:, t, 6 * h:6 * h + 6], vm[:, t * DA + h * BANK:t * DA + (h + 1) * BANK])
                after(last)
                after(nc.vector.bn_aggr(mv[:, t, :], bn[:, t, :]))
                nc.vector.tensor_scalar(ln_var[:, t:t + 1], mv[:, t, 1:2], EPS, None, ALU.add).then_inc(v_var_ready, 1)
            dve.wait_ge(lngb_landed, 32)
            for t in range(T):
                dve.wait_ge(v_rs_ready, t + 1)
                vt = vm[:, t * DA:(t + 1) * DA]
                after(nc.vector.tensor_scalar(vt, vt, mv[:, t, 0:1], ln_rs[:, t:t + 1], ALU.subtract, ALU.mult))
                after(nc.vector.tensor_tensor(vt, vt, tok[:, 0:DA], ALU.mult))
                nc.vector.tensor_tensor(vt, vt, tok[:, DA:D], ALU.add).then_inc(v_normed, 1)
                if t == 0:
                    split(Q_A + 1, 0, ab + 4)
                    split(Q_A + 1, 1, ab + 5)
            split(Q_A + 1, 2, ab + 6)
            split(Q_A + 1, 3, ab + 7)
            for t in range(T):
                dve.wait_ge(v_hi_ready, t + 1)
                dve.wait_ge(v_normed, t + 1)
                nc.vector.tensor_tensor(vd_lo[:, t * DA:(t + 1) * DA], vm[:, t * DA:(t + 1) * DA],
                                        vd_hi[:, t * DA:(t + 1) * DA], ALU.subtract).then_inc(v_lo_ready, 1)
            split_quad(Q_A + 2, ab, 8)
            dve.wait_ge(bs_landed, 16)
            dve.wait_ge(v_lo_ready, 2)
            split_quad(Q_A + 3, ab, 12)
            for h in range(HEADS):
                dve.wait_ge(mixed_ready, h + 1)
                nc.vector.tensor_tensor(vm[:, h * BANK:(h + 1) * BANK].rearrange("p (k n) -> p k n", n=P), pairs(h),
                                        bs[:, h:h + 1, :].to_broadcast([P, 4, P]), ALU.add).then_inc(mixed_kept, 1)
            split_quad(Q_U, ab, 0)
            for t in range(T):
                for h in range(2):
                    n = t * 4 + h * 2
                    dve.wait_ge(a_hi_ready, 2 * t + h + 1)
                    nc.vector.tensor_tensor(mix_lo[:, 8 + n:10 + n, :], acc[:, 4 + 2 * t + h, :].rearrange(
                        "p (k n) -> p k n", n=SEQ), mix_hi[:, 8 + n:10 + n, :], ALU.subtract).then_inc(a_lo_ready, 1)
            split_quad(Q_U + 1, ab, 4)
            for g in range(4):
                dve.wait_ge(pd_hi_ready, g + 1)
                nc.vector.tensor_tensor(vd_lo[:, g * BANK:(g + 1) * BANK], acc[:, 4 + g, :],
                                        vd_hi[:, g * BANK:(g + 1) * BANK], ALU.subtract).then_inc(pd_lo_ready, 1)
            split_quad(Q_U + 2, ab, 8)
            for g in range(4):
                dve.wait_ge(ga_hi_ready, g + 1)
                for n in range(2):
                    k = 2 * g + n
                    last = nc.vector.scalar_tensor_tensor(mix_lo[:, k, :], acc[:, 4 + g, n * SEQ:(n + 1) * SEQ],
                                                          vecs[:, V_ASCALE + k:V_ASCALE + k + 1], mix_hi[:, k, :],
                                                          ALU.mult, ALU.subtract)
                last.then_inc(ga_lo_ready, 1)
            split_quad(Q_U + 3, ab, 12)
            split_quad(Q_OUT)
            dve.wait_ge(mixed_kept, HEADS)
            for g in range(4):
                dve.wait_ge(u_gelu, g + 1)
                nc.vector.tensor_tensor(vm[:, g * BANK:(g + 1) * BANK], acc[:, g, :], vm[:, g * BANK:(g + 1) * BANK],
                                        ALU.mult).then_inc(gated_ready, 1)
            for g in range(4):
                dve.wait_ge(gb_hi_ready, g + 1)
                nc.vector.tensor_tensor(mix_lo[:, 8 + 2 * g:10 + 2 * g, :], vm[:, g * BANK:(g + 1) * BANK].rearrange(
                    "p (k n) -> p k n", n=SEQ), mix_hi[:, 8 + 2 * g:10 + 2 * g, :], ALU.subtract).then_inc(gb_lo_ready, 1)
            for k in range(1, 5):
                split_quad(Q_OUT + k)
            gain_y(0, 0, 0, (0, 1))
            gain_y(0, 0, 1, (0, 1))
            for k in range(5, 8):
                split_quad(Q_OUT + k)
            open_ffn(0, 0, Q_F0, V_PRE["f0"])

            def ffn(layer, q0, gain, par, e):
                dve.wait_ge(x_rs_ready, 2 * (e - 1) + 4)

                def hidden(i, bank_par, t):
                    dve.wait_ge(silu_ready, i * 2 + (22 * layer + t + 1))
                    nc.vector.scalar_tensor_tensor(tok[:, t * DA:t * DA + BANK], acc[:, 4 * bank_par + 2 * t + 1, :],
                                                   x_rs[:, t:t + 1], tok[:, t * DA + BANK:(t + 1) * DA],
                                                   ALU.mult, ALU.mult).then_inc(hid_ready, 1)

                def lo_hid(i, bank_par, t):
                    dve.wait_ge(hT_hi_ready, i * 2 + (22 * layer + t + 1))
                    nc.vector.tensor_tensor(hT_lo[:, bass.ts(i, 4), t * P:(t + 1) * P], pairs(4 * bank_par + 2 * t),
                                            hT_hi[:, bass.ts(i, 4), t * P:(t + 1) * P], ALU.subtract).then_inc(hT_lo_ready, 1)

                def chunk(i, bank_par):
                    split_quad(i * 4 + q0, gain, 0)
                    hidden(i - 1, bank_par, 0)
                    hidden(i - 1, bank_par, 1)
                    split_quad(i * 4 + (q0 + 1), gain, 4)
                    lo_hid(i - 1, bank_par, 0)
                    lo_hid(i - 1, bank_par, 1)
                    split_quad(i * 4 + (q0 + 2), gain, 8)
                    split_quad(i * 4 + (q0 + 3), gain, 12)

                with dve.Fori(0, (FFC - 1) // 2) as n:
                    chunk(n * 2 + 1, par)
                    chunk(n * 2 + 2, 1 - par)
                qd = q0 + Q_FF
                split_quad(qd)
                hidden(FFC - 1, par, 0)
                hidden(FFC - 1, par, 1)
                split_quad(qd + 1)
                lo_hid(FFC - 1, par, 0)
                lo_hid(FFC - 1, par, 1)
                with dve.Fori(qd + 2, qd + Q_DOWN // 2 + 1) as q:
                    split_quad(q)
                gain_y(e, par, 0, (0, 1))
                gain_y(e, par, 1, (0, 1))
                with dve.Fori(qd + Q_DOWN // 2 + 1, qd + Q_DOWN) as q:
                    split_quad(q)

            ffn(0, Q_F0, V_PRE["f0"], 1, 1)
            c_gain = V_PRE["c"]
            gain_y(1, 1, 0, (2, 3))
            mean_square(y_sums, y_var, 0, y_square(1, 0, 3) + 1, y_var_ready)
            add_y(1, 1, 0, range(4))
            mean_square(x_sums, x_var, 0, x_square(2, 0, 3) + 1, x_var_ready)
            gain_y(1, 1, 1, (2, 3))
            mean_square(y_sums, y_var, 1, y_square(1, 1, 3) + 1, y_var_ready)
            split(Q_PW1, 0)
            add_y(1, 1, 1, range(4))
            mean_square(x_sums, x_var, 1, x_square(2, 1, 3) + 1, x_var_ready)
            lo_xT(2, 1, 0, range(4), c_gain)
            split(Q_PW1, 1)
            lo_xT(2, 1, 1, range(4), c_gain)
            split(Q_PW1, 2)
            split(Q_PW1, 3)

            dve.wait_ge(consts_set, 5)
            dve.wait_ge(taps_landed, 16)

            def glu(c, par, g):
                dve.wait_ge(gate_ready, c + 1)
                for n in range(2):
                    nc.vector.tensor_tensor(g[:, n, PAD:], lin[:, par, n, :], sig[:, par, n, :], ALU.mult).then_inc(glu_ready, 1)

            def convolve(c):
                for n in range(2):
                    nc.vector.tensor_copy(taps_now[:, n, :], taps[:, bass.ds(c * 2 + n, 1), :].rearrange(
                        "p a n -> p (a n)")).then_inc(taps_copied, 1)
                dve.wait_ge(taps_copied, c * 2 + 2)
                for j in range(TAPS):
                    for n in range(2):
                        m = acc[:, 2, n * SEQ:(n + 1) * SEQ]
                        src = g_now[:, n, j:j + SEQ]
                        w = taps_now[:, n, j:j + 1]
                        if j == 0:
                            dve.wait_ge(glu_ready, c * 2 + (n + 1))
                            nc.vector.tensor_scalar(m, src, w, vecs[:, bass.ds(V_BDW + c * 2 + n, 1)],
                                                    ALU.mult, ALU.add).then_inc(tap_done, 1)
                            continue
                        dve.wait_ge(tap_done, c * (2 * (TAPS - 1)) + (2 * (j - 1) + n + 1))
                        if j < TAPS - 1:
                            nc.vector.scalar_tensor_tensor(m, src, w, m, ALU.mult, ALU.add).then_inc(tap_done, 1)
                        else:
                            nc.vector.scalar_tensor_tensor(conv[:, bass.ds(c * 2 + n, 1), :].rearrange("p a n -> p (a n)"),
                                                           src, w, m, ALU.mult, ALU.add).then_inc(conv_ready, 1)

            def chunk(c, par):
                if not isinstance(c, int) or c:
                    dve.wait_ge(conv_ready, c * 2)
                glu(c, par, g_now)
                convolve(c)

            def lo_c(c):
                dve.wait_ge(cT_hi_ready, c + 1)
                nc.vector.tensor_tensor(cT_lo[:, 2 * c:2 * c + 2, :], conv[:, 2 * c:2 * c + 2, :],
                                        cT_hi[:, 2 * c:2 * c + 2, :], ALU.subtract).then_inc(cT_lo_ready, 1)

            chunk(0, 0)
            chunk(1, 1)
            with dve.Fori(1, CCH // 2 - 1) as i:
                chunk(i * 2, 0)
                chunk(i * 2 + 1, 1)
            dve.wait_ge(conv_ready, 2 * (CCH - 2))
            glu(CCH - 2, 0, g_now)
            glu(CCH - 1, 1, g_last)
            split_quad(Q_PW2)
            convolve(CCH - 2)
            dve.wait_ge(sq_used, CCH)
            after(nc.vector.tensor_copy(cst[:].rearrange("p t n -> p (t n)"), acc[:, 6, 0:2 * T]))
            after(nc.vector.tensor_tensor(cvar[:, :, 0], cst[:, :, 0], cst[:, :, 0], ALU.mult))
            after(nc.vector.tensor_tensor(cvar[:, :, 1], cst[:, :, 1], cvar[:, :, 0], ALU.subtract))
            nc.vector.tensor_scalar(cvar[:, :, 1], cvar[:, :, 1], 0.0, EPS, ALU.max, ALU.add).then_inc(cvar_ready, 1)
            for t in range(T):
                last = nc.vector.tensor_scalar(diag[:, 0, t * P:(t + 1) * P], ident[:], cst[:, t, 0:1], None, ALU.mult)
            last.then_inc(cst_diag_ready, 1)
            dve.wait_ge(crs_ready, 1)
            for t in range(T):
                last = nc.vector.tensor_scalar(diag[:, 1, t * P:(t + 1) * P], ident[:], crs[:, t:t + 1], None, ALU.mult)
            last.then_inc(cst_diag_ready, 1)
            for c in range(CCH):
                cs = conv[:, 2 * c:2 * c + 2, :]
                dve.wait_ge(cst_spread, 1)
                after(nc.vector.tensor_tensor(cs, cs, acc[:, 7:8, 0:SEQ].to_broadcast([P, 2, SEQ]), ALU.subtract))
                dve.wait_ge(cst_spread, 2)
                nc.vector.tensor_tensor(cs, cs, acc[:, 6:7, 0:SEQ].to_broadcast([P, 2, SEQ]),
                                        ALU.mult).then_inc(c_normed, 1)
                if c:
                    lo_c(c - 1)
            lo_c(CCH - 1)
            for k in range(1, 5):
                split_quad(Q_PW2 + k)
            gain_y(2, 1, 0, (0, 1))
            gain_y(2, 1, 1, (0, 1))
            for k in range(5, 8):
                split_quad(Q_PW2 + k)
            open_ffn(2, 1, Q_F1, V_PRE["f1"])
            ffn(1, Q_F1, V_PRE["f1"], 0, 3)
            for t in range(T):
                gain_y(3, 0, t, (2, 3))
                mean_square(y_sums, y_var, t, y_square(3, t, 3) + 1, y_var_ready)
                add_y(3, 0, t, range(4))

        @block.tensor
        def _(pe):
            mm = nc.tensor.matmul

            def wait_split(q, s):
                if isinstance(q, int) and q >= Q_POOL1:
                    pe.wait_ge(lo_ready, lo_count(q, s, True))
                elif isinstance(q, int) and q >= Q_POOL0:
                    pe.wait_ge(lo_ready_pool, lo_pool_count(q, s))
                else:
                    pe.wait_ge(lo_ready, lo_count(q, s))

            def unit_by_token(s, lhs_hi, lhs_lo, k, par, t, start, stop):
                xh, xl = lhs_hi[:, k, t * P:(t + 1) * P], lhs_lo[:, k, t * P:(t + 1) * P]
                for xs, ws in ((xh, w_hi), (xh, w_lo), (xl, w_hi)):
                    for h in range(2):
                        last = mm(acc[:, 4 * par + 2 * t + h, :], xs, ws[:, s, h * BANK:(h + 1) * BANK],
                                  start=start and ws is w_hi and xs is xh, stop=stop and xs is xl)
                return last

            def block_by_channel(s, col, k, bank, half, start, stop):
                out = acc[:, bank, half * SEQ:(half + 1) * SEQ]
                wh, wl = w_hi[:, s, col:col + P], w_lo[:, s, col:col + P]
                mm(out, wh, xT_hi[:, k, :], start=start and half == 0, stop=False, skip_group_check=True)
                mm(out, wh, xT_lo[:, k, :], start=False, stop=False, skip_group_check=True)
                return mm(out, wl, xT_hi[:, k, :], start=False, stop=stop, skip_group_check=True)

            def quad(q, lhs_hi, lhs_lo, k0, par, start=False, stop=None, wait=None, after_pool=False, by_tile=False):
                order = [(t, s) for t in range(T) for s in range(4)] if by_tile else [(t, s) for s in range(4) for t in range(T)]
                for t, s in order:
                    if t == 0:
                        if after_pool:
                            pe.wait_ge(lo_ready, lo_count(q, s, True))
                        else:
                            wait_split(q, s)
                    if wait is not None:
                        wait(t, s)
                    last = unit_by_token(s, lhs_hi, lhs_lo, k0 + s, par, t, start and s == 0, stop is not None and s == 3)
                    if t == T - 1:
                        last.then_inc(units_used, 1)
                    elif stop is not None and s == 3:
                        last.then_inc(stop, 1)

            def turn_x(b, par, t, cs):
                for c in cs:
                    if b % 2:
                        pe.wait_ge(x_ready, x_place(b, t, c) - 7)
                    else:
                        pe.wait_ge(xn_ready, 4 * b + 4 * t + c + 1)
                    for n in range(4):
                        k = 4 * c + n
                        src = x[:, t, k * P:(k + 1) * P] if b % 2 else tok[:, k * P:(k + 1) * P]
                        last = nc.tensor.transpose(pairs(y_bank(par, t, c))[:, n, :], src, ident[:])
                    last.then_inc(xn_turned, 1)

            def open_stage(q, b, y_par, par, cs, after_pool=False):
                for t in range(T):
                    turn_x(b, y_par, t, cs)
                    for s in range(4):
                        if t == 0:
                            if after_pool:
                                pe.wait_ge(lo_ready, lo_count(q, s, True))
                            else:
                                wait_split(q, s)
                        if s == 0:
                            pe.wait_ge(xT_lo_ready, x_place(b, t, 1) + 1)
                        last = unit_by_token(s, xT_hi, xT_lo, s, par, t, s == 0, False)
                        if t == T - 1:
                            last.then_inc(units_used, 1)

            def x_quads(q, b, y_par, par, stop, after_pool=False):
                for c in range(1, 4):
                    pe.wait_ge(xT_lo_ready, x_place(b, 1, c) + 1)
                    quad(q + c, xT_hi, xT_lo, 4 * c, par, stop=stop if c == 3 else None, after_pool=after_pool)
                    if c == 1 and b % 2:
                        for t in range(T):
                            turn_x(b, y_par, t, (2, 3))

            pe.wait_ge(ident_landed, 16)
            open_stage(Q_V, 0, 1, 0, range(4))
            x_quads(Q_V, 0, 1, 0, in0_ready)
            for c in range(4):
                quad(Q_A + c, xT_hi, xT_lo, 4 * c, 1, start=c == 0, stop=in0_ready if c == 3 else None)
                if c == 2:
                    for k in range(8):
                        h = k // 2
                        for t in range(T):
                            pe.wait_ge(v_lo_ready, t + 1)
                            out = acc[:, h, (k % 2) * SEQ + t * P:(k % 2) * SEQ + (t + 1) * P]
                            vs = slice(t * DA + k * P, t * DA + (k + 1) * P)
                            ws = slice(BANK + h * P, BANK + (h + 1) * P)
                            mm(out, vd_hi[:, vs], c_hi[:, 3, ws], start=True, stop=False)
                            mm(out, vd_hi[:, vs], c_lo[:, 3, ws], start=False, stop=False)
                            last = mm(out, vd_lo[:, vs], c_hi[:, 3, ws], start=False, stop=True)
                        if k % 2:
                            last.then_inc(mixed_ready, 1)
            pe.wait_ge(mixed_kept, HEADS)
            for c in range(4):
                for s in range(4):
                    wait_split(Q_U + c, s)
                    for k in range(8):
                        last = block_by_channel(s, k * P, 4 * c + s, k // 2, k % 2, c == 0 and s == 0, c == 3 and s == 3)
                    last.then_inc(units_used, 1)
                if c == 0:
                    pe.wait_ge(a_lo_ready, 4)
                    for k in range(8):
                        g = k // 2
                        out = acc[:, 4 + g, (k % 2) * SEQ:(k % 2 + 1) * SEQ]
                        for t in range(T):
                            a = 8 + 4 * t + k // 2
                            ac = slice((k % 2) * P, (k % 2 + 1) * P)
                            band = (2, slice(g * SEQ, (g + 1) * SEQ)) if t == 0 else (3, slice(g * P, (g + 1) * P))
                            o = out if t == 0 else out[:, P:SEQ]
                            mm(o, mix_hi[:, a, ac], c_hi[:, band[0], band[1]], start=t == 0, stop=False, skip_group_check=True)
                            mm(o, mix_hi[:, a, ac], c_lo[:, band[0], band[1]], start=False, stop=False, skip_group_check=True)
                            last = mm(o, mix_lo[:, a, ac], c_hi[:, band[0], band[1]], start=False, stop=t == 1,
                                      skip_group_check=True)
                        if k % 2:
                            last.then_inc(pooled_ready, 1)
                if c == 1:
                    for g in range(4):
                        pe.wait_ge(pd_lo_ready, g + 1)
                        for n in range(2):
                            out = acc[:, 4 + g, n * SEQ:(n + 1) * SEQ]
                            for cb in range(2):
                                w0 = (g % 2) * 2 * SEQ + cb * SEQ + n * P
                                ws = slice(w0, w0 + P)
                                ds = slice((2 * g + cb) * SEQ, (2 * g + cb + 1) * SEQ)
                                mm(out, c_hi[:, g // 2, ws], vd_hi[:, ds], start=cb == 0, stop=False)
                                mm(out, c_hi[:, g // 2, ws], vd_lo[:, ds], start=False, stop=False)
                                last = mm(out, c_lo[:, g // 2, ws], vd_hi[:, ds], start=False, stop=cb == 1)
                        last.then_inc(group_ready, 1)
            pe.wait_ge(ga_lo_ready, 4)
            for j in range(2):
                for c in range(4):
                    if j == 0 and c >= 2:
                        pe.wait_ge(gb_lo_ready, 2 * c - 2)
                    quad(Q_OUT + 4 * j + c, mix_hi, mix_lo, 4 * c, 1 - j, start=c == 0, stop=y0_ready if c == 3 else None,
                         by_tile=j == 1 and c == 3)

            def ffn(layer, q0, b, y_par, par):
                pool = layer == 1
                open_stage(q0, b, y_par, par, (0, 1), pool)
                x_quads(q0, b, y_par, par, gu0_ready, pool)

                def turn_hidden(i, bank_par):
                    for t in range(T):
                        pe.wait_ge(hid_ready, i * 2 + (22 * layer + t + 1))
                        for n in range(4):
                            last = nc.tensor.transpose(pairs(4 * bank_par + 2 * t)[:, n, :],
                                                       tok[:, t * DA + n * P:t * DA + (n + 1) * P], ident[:])
                        last.then_inc(hid_turned, 1)

                def chunk(i, bank_par):
                    for c in range(4):
                        quad(i * 4 + (q0 + c), xT_hi, xT_lo, 4 * c, bank_par, start=c == 0,
                             stop=gu0_ready if c == 3 else None, after_pool=pool)
                        if c == 0:
                            turn_hidden(i - 1, 1 - bank_par)

                with pe.Fori(0, (FFC - 1) // 2) as n:
                    chunk(n * 2 + 1, 1 - par)
                    chunk(n * 2 + 2, par)
                qd = q0 + Q_FF
                pe.wait_ge(hT_lo_ready, 22 * layer + 20)
                for j in range(2):
                    for c in range(FFC):
                        if j == 0:
                            pe.wait_ge(hT_lo_ready, 22 * layer + 2 * (c + 1))
                        quad(qd + j * FFC + c, hT_hi, hT_lo, 4 * c, par if j else 1 - par, start=c == 0,
                             stop=y0_ready if c == FFC - 1 else None, after_pool=pool, by_tile=j == 1 and c == FFC - 1)
                        if j == 0 and c == 0:
                            turn_hidden(FFC - 1, par)

            ffn(0, Q_F0, 1, 0, 1)

            for t in range(T):
                turn_x(2, 1, t, range(4))

            def conv_in(c, par, dynamic=True):
                for u in range(8):
                    s = u % 4
                    q = c * 2 + (Q_PW1 + u // 4)
                    if u < 4 and not dynamic and c == 0:
                        pe.wait_ge(lo_ready, lo_count(Q_PW1, s))
                    else:
                        pe.wait_ge(lo_ready_pool, lo_pool_count(q, s))
                    if not dynamic and c == 0 and u % 2 == 0:
                        pe.wait_ge(xT_lo_ready, x_place(2, 1, u // 2) + 1)
                    for kk in range(2):
                        k = 2 * u + kk
                        for n in range(4):
                            last = block_by_channel(s, kk * 2 * CC + n * P, k, 4 * par + n % 2, n // 2, k == 0, k == KT - 1)
                    last.then_inc(units_used, 1)

            conv_in(0, 0, False)
            conv_in(1, 1, False)
            with pe.Fori(1, CCH // 2) as i:
                pe.wait_ge(gate_ready, i * 2 - 1)
                conv_in(i * 2, 0)
                pe.wait_ge(gate_ready, i * 2)
                conv_in(i * 2 + 1, 1)

            def sum_channels(place, c):
                if c == CCH - 1:
                    pe.wait_ge(conv_last_ready, 2)
                else:
                    pe.wait_ge(conv_ready, 2 * (c + 1))
                for square in range(2):
                    if square:
                        pe.wait_ge(sq_ready, place + 1)
                    for n in range(2):
                        src = sq[:, place % 2, n, :] if square else conv[:, 2 * c + n, :]
                        for t in range(T):
                            last = mm(acc[:, 6, 2 * t + square:2 * t + square + 1], src[:, t * P:(t + 1) * P], one_mean[:],
                                      start=place + square + n + t == 0, stop=place == CCH - 1 and n == 1,
                                      skip_group_check=True)
                last.then_inc(sq_used, 1)

            pe.wait_ge(consts_set, 5)
            for place in range(5):
                sum_channels(place, SQ_ORDER[place])
            for i in range(2 * TAPS):
                pe.wait_ge(prod_ready, i + 1)
                mm(acc[:, 3, (i % 2) * SEQ:(i % 2 + 1) * SEQ], ident[:], prod[:, i % 4, :], start=i == 0,
                   stop=i >= 2 * TAPS - 2, skip_group_check=True).then_inc(prod_used, 1)
            for place in range(5, CCH):
                sum_channels(place, SQ_ORDER[place])
            for i in range(2):
                pe.wait_ge(cst_diag_ready, i + 1)
                mm(acc[:, 7 - i, 0:SEQ], ones[:], diag[:, i, :], start=True, stop=True).then_inc(cst_spread, 1)
            pe.wait_ge(bpw2_landed, 16)
            for j in range(2):
                for t in range(T):
                    for h in range(2):
                        mm(acc[:, 4 * j + 2 * t + h, :], ones[0:1, :], tok[0:1, j * UNIT + h * BANK:j * UNIT + (h + 1) * BANK],
                           start=True, stop=False)
                for c in range(4):
                    if j == 0:
                        pe.wait_ge(cT_lo_ready, 2 * c + 2)
                    quad(Q_PW2 + 4 * j + c, cT_hi, cT_lo, 4 * c, j, stop=y0_ready if c == 3 else None,
                         by_tile=j == 1 and c == 3)
            ffn(1, Q_F1, 3, 1, 0)


def bands():
    out = np.zeros((P, 4 * SEQ + 4 * P), np.float32)
    s, t = np.arange(SEQ)[:, None], np.arange(SEQ)[None, :]
    for g, w in enumerate(WINDOWS):
        m = np.where((t >= s) & (t - s < w), np.float32(1) / np.minimum(t + 1, w).astype(np.float32), np.float32(0))
        m = m.astype(np.float32) - (s == t).astype(np.float32)
        out[:, g * SEQ:(g + 1) * SEQ] = m[:P]
        out[:, 4 * SEQ + g * P:4 * SEQ + (g + 1) * P] = m[P:, P:]
    return out


def by_k(w, cols):
    k, n = w.shape
    return w.reshape(k // P, P, n // cols, cols).transpose(2, 0, 1, 3)


def weight_units(ab_w_in, a_w_group, b_w_s, ab_w_out, c_w_pw1, c_w_pw2, f_w_gate, f_w_up, f_w_down):
    band = bands()
    groups = a_w_group[0].reshape(4, 2, P, 2 * P).transpose(2, 0, 1, 3).reshape(P, 2, UNIT).transpose(1, 0, 2)
    spatial = b_w_s[0].transpose(2, 0, 1).reshape(P, HEADS * P)
    w_in = by_k(ab_w_in[0], UNIT)
    out = [w_in[2], groups, band[None, :, :UNIT], np.concatenate([band[:, UNIT:], spatial], axis=1)[None],
           w_in[0], w_in[1]]

    def ffn(i):
        gate_up = np.concatenate([by_k(f_w_gate[i], BANK), by_k(f_w_up[i], BANK)], axis=3)
        return [gate_up.reshape(-1, P, UNIT), by_k(f_w_down[i], UNIT).reshape(-1, P, UNIT)]

    out += [by_k(ab_w_out[0], UNIT).reshape(-1, P, UNIT)] + ffn(0)
    pw1 = c_w_pw1[0].reshape(KT // 2, 2, P, 2, CCH, CC).transpose(4, 0, 2, 1, 3, 5)
    out += [pw1.reshape(-1, P, UNIT), by_k(c_w_pw2[0], UNIT).reshape(-1, P, UNIT)] + ffn(1)
    return np.concatenate([np.asarray(a, np.float32).reshape(-1, P, UNIT) for a in out])


def columns(v):
    return v.reshape(-1, P).T


def kernel(x, ab_norm_pre, ab_w_in, a_w_group, a_scale, b_ln_g, b_ln_b, b_w_s, b_b_s, ab_w_out, ab_norm_post,
           c_norm_pre, c_w_pw1, c_b_pw1, c_w_dw, c_b_dw, c_ln_g, c_ln_b, c_w_pw2, c_b_pw2, c_norm_post,
           f_norm_pre, f_w_gate, f_w_up, f_w_down, f_norm_post):
    import concourse.bacc as bacc
    from concourse.bass_utils import run_bass_kernel_spmd

    a = [np.asarray(v) for v in (ab_w_in, a_w_group, b_w_s, ab_w_out, c_w_pw1, c_w_pw2, f_w_gate, f_w_up, f_w_down)]
    vecs = [ab_norm_pre[0], f_norm_pre[0], c_norm_pre[0], f_norm_pre[1], a_scale[0], c_b_pw1[0], c_b_dw[0],
            c_ln_g[0], c_ln_b[0]]
    arrays = {
        "x": np.asarray(x)[0],
        "units": weight_units(*a),
        "vecs": np.concatenate([columns(np.asarray(v)) for v in vecs], axis=1),
        "taps": np.asarray(c_w_dw)[0].reshape(TAPS, KT, P).transpose(2, 1, 0),
        "ident": np.eye(P, dtype=np.float32),
        "bs": np.asarray(b_b_s),
        "lng": np.asarray(b_ln_g),
        "lnb": np.asarray(b_ln_b),
        "bpw2": np.asarray(c_b_pw2),
        "post": np.stack([np.asarray(v) for v in (ab_norm_post[0], f_norm_post[0], c_norm_post[0], f_norm_post[1])]),
    }
    arrays = {n: np.ascontiguousarray(v) for n, v in arrays.items()}
    nc = bacc.Bacc("TRN2", target_bir_lowering=False, num_devices=1)
    args = [nc.dram_tensor("in_" + n, v.shape, mybir.dt.from_np(v.dtype), kind="ExternalInput").ap() for n, v in arrays.items()]
    out = nc.dram_tensor("out", (SEQ, D), F32, kind="ExternalOutput").ap()
    trunk(nc, *args, out)
    r = run_bass_kernel_spmd(nc, [{"in_" + n: v for n, v in arrays.items()}], core_ids=[0])
    return r.results[0]["out"].reshape(1, SEQ, D)
```

```python
from contextlib import ExitStack

import concourse.bass as bass
import numpy as np
from concourse import mybir

F32 = mybir.dt.float32
F32R = mybir.dt.float32r
ALU = mybir.AluOpType
ACT = mybir.ActivationFunctionType
AX = mybir.AxisListType

P = 128
D = 2048
SEQ = 256
T = SEQ // P
KT = D // P
DA = D // 2
DFF = 5632
FT = DFF // P
WINDOWS = (2, 4, 8, 16)
HEADS = 4
TAPS = 31
PAD = TAPS - 1
EPS = 1e-6
UNIT = 1024
BANK = 512
FFC = DFF // BANK
CC = 256
CCH = D // CC

Q_V = 0
Q_CONST = 4
Q_A = 5
Q_U = 9
Q_OUT = 13
Q_F0 = Q_OUT + 8
Q_FF = FFC * KT // 4
Q_DOWN = 2 * FT // 4
Q_PW1 = Q_F0 + Q_FF + Q_DOWN
Q_PW2 = Q_PW1 + CCH * KT // 2 // 4
Q_F1 = Q_PW2 + 8
Q_END = Q_F1 + Q_FF + Q_DOWN
Y_LAST = [(Q_OUT + 3, Q_OUT + 7), (Q_F0 + Q_FF + FFC - 1, Q_PW1 - 1), (Q_PW2 + 3, Q_F1 - 1), (Q_F1 + Q_FF + FFC - 1, Q_END - 1)]
SQ_ORDER = [0, 1, 2, 3, 4, 5, CCH - 1, CCH - 2]
SQ_POOL = CCH - 2
Q_POOL0, Q_POOL1 = Q_PW1, Q_PW2 + 1

V_PRE = {"ab": 0, "f0": 16, "c": 32, "f1": 48}
V_ASCALE = 64
V_BA, V_BG, V_BDW, V_LNG, V_LNB = 72, 88, 104, 120, 136
V_ALL = 152


def hi_count(q, s):
    return q * 4 + (s + 1)


def used_count(q, s):
    before_consts = isinstance(q, int) and q < Q_CONST
    return (q if before_consts else q - 1) * 4 + (s + 1)


def lo_count(q, s, after_pool=False):
    return (q - (Q_POOL1 - Q_POOL0 if after_pool else 0)) * 4 + (s + 1)


def y_square(e, t, c):
    at = 2 * t + c if c < 2 else 2 + c + t * (6 if e == 1 else 2)
    return 8 + 16 * e + at


def x_square(b, t, c):
    if b == 0:
        return 4 * t + c
    return 8 + 16 * (b - 1) + (6 * (t + 1) + c if b == 2 else 8 + 4 * t + c)


def by_tile_halves(t, c):
    return 4 * (c // 2) + 2 * t + c % 2


def added(b, t, c):
    return 8 * (b - 1) + (4 * t + c if b % 2 == 0 else by_tile_halves(t, c)) + 1


def turned(b, t, c):
    return 8 * b + (2 * c + t if b == 0 else 4 * t + c if b == 2 else by_tile_halves(t, c)) + 1


def parted(b, t, c):
    return 8 * b + (2 * c + t if b == 0 else by_tile_halves(t, c)) + 1


def lo_pool_count(q, s):
    return (q - Q_POOL0) * 4 + (s + 1)


def trunk(nc, d_x, d_units, d_vecs, d_taps, d_ident, d_bs, d_lng, d_lnb, d_bpw2, d_post, d_out):
    with ExitStack() as ctx:
        sb = lambda name, shape, dt=F32: ctx.enter_context(nc.sbuf_tensor(name, shape, dt))
        sem = lambda name: ctx.enter_context(nc.semaphore(name))

        x = sb("x", [P, T, D])
        xT_hi = sb("xT_hi", [P, KT, SEQ], F32R)
        xT_lo = sb("xT_lo", [P, KT, SEQ], F32R)
        raw = sb("raw", [P, 4, UNIT])
        w_hi = sb("w_hi", [P, 4, UNIT], F32R)
        w_lo = sb("w_lo", [P, 4, UNIT], F32R)
        gpost = sb("gpost", [P, D])
        tok = sb("tok", [P, D])
        junk = sb("junk", [P, 2, BANK], mybir.dt.bfloat16)
        vecs = sb("vecs", [P, V_ALL])
        ident = sb("ident", [P, P])
        warm = sb("warm", [P, 1])
        ones = sb("ones", [P, P])
        rs_row = sb("rs_row", [P, 1, SEQ])
        pow_exp = sb("pow_exp", [P, 1])
        y_sums = sb("y_sums", [P, T, 4])
        x_sums = sb("x_sums", [P, T, 4])
        y_var = sb("y_var", [P, T, 2])
        x_var = sb("x_var", [P, T, 2])
        y_rs = sb("y_rs", [P, T])
        x_rs = sb("x_rs", [P, T])
        rs_diag = tok[:, 0:T * P].rearrange("p (t n) -> p t n", n=P)
        acc = ctx.enter_context(nc.psum_tensor("acc", [P, 8, BANK], F32))

        with ExitStack() as m:
            mb = lambda name, shape, dt=F32: m.enter_context(nc.sbuf_tensor(name, shape, dt))
            mix_hi = mb("mix_hi", [P, KT, SEQ], F32R)
            mix_lo = mb("mix_lo", [P, KT, SEQ], F32R)
            vm = mb("vm", [P, D])
            vd_hi = mb("vd_hi", [P, D], F32R)
            vd_lo = mb("vd_lo", [P, D], F32R)
            c_hi = mb("c_hi", [P, 4, UNIT], F32R)
            c_lo = mb("c_lo", [P, 4, UNIT], F32R)
            bs = mb("bs", [P, HEADS, P])
            bn = mb("bn", [P, T, 12])
            mv = mb("mv", [P, T, 2])
            ln_var = mb("ln_var", [P, T])
            ln_rs = mb("ln_rs", [P, T])
        with ExitStack() as m:
            mb = lambda name, shape, dt=F32: m.enter_context(nc.sbuf_tensor(name, shape, dt))
            cT_hi = mb("cT_hi", [P, KT, SEQ], F32R)
            cT_lo = mb("cT_lo", [P, KT, SEQ], F32R)
            conv = mb("conv", [P, KT, SEQ])
            taps = mb("taps", [P, KT, TAPS])
            taps_now = mb("taps_now", [P, 2, TAPS])
            g_now = mb("g_now", [P, 2, PAD + SEQ])
            g_tail = mb("g_tail", [P, 2, 2, PAD + SEQ])
            sig = mb("sig", [P, 2, 2, SEQ])
            lin = mb("lin", [P, 2, 2, SEQ])
            sq = mb("sq", [P, 2, 2, SEQ])
            prod = mb("prod", [P, 4, SEQ])
            conv_sum = mb("conv_sum", [P, 2, SEQ])
            sq_sum = mb("sq_sum", [P, 2, SEQ])
            one_mean = mb("one_mean", [P, 1])
            cst = mb("cst", [P, T, 2])
            cvar = mb("cvar", [P, T, 2])
            crs = mb("crs", [P, T])
            diag = mb("diag", [P, 2, SEQ])
            bias_rows = mb("bias_rows", [2 * 32, D], F32R)
            ones_r = mb("ones_r", [2 * 32, P], F32R)
        with ExitStack() as m:
            mb = lambda name, shape, dt=F32: m.enter_context(nc.sbuf_tensor(name, shape, dt))
            hT_hi = mb("hT_hi", [P, FT, SEQ], F32R)
            hT_lo = mb("hT_lo", [P, FT, SEQ], F32R)

        raw_landed = [sem(f"raw_landed{s}") for s in range(4)]
        x_landed = [[sem(f"x_landed{t}{h}") for h in range(2)] for t in range(T)]
        vecs_landed = sem("vecs_landed")
        ident_landed = sem("ident_landed")
        post_landed = sem("post_landed")
        bs_landed = sem("bs_landed")
        lngb_landed = sem("lngb_landed")
        taps_landed = sem("taps_landed")
        bpw2_landed = sem("bpw2_landed")
        bias_cleared = sem("bias_cleared")
        bias_hi_ready = sem("bias_hi_ready")
        bias_lo_ready = sem("bias_lo_ready")
        out_stored = sem("out_stored")
        hi_ready = sem("hi_ready")
        lo_ready = sem("lo_ready")
        lo_ready_pool = sem("lo_ready_pool")
        units_used = sem("units_used")
        consts_set = sem("consts_set")
        w_s_masked = sem("w_s_masked")
        y0_ready = sem("y0_ready")
        y2_ready = sem("y2_ready")
        squared = sem("squared")
        y_gained = sem("y_gained")
        y_var_ready = sem("y_var_ready")
        y_rs_ready = sem("y_rs_ready")
        x_ready = sem("x_ready")
        x_var_ready = sem("x_var_ready")
        x_rs_ready = sem("x_rs_ready")
        rs_diag_ready = sem("rs_diag_ready")
        rs_spread = sem("rs_spread")
        rs_row_ready = sem("rs_row_ready")
        x_turned = sem("x_turned")
        xT_hi_ready = sem("xT_hi_ready")
        xT_lo_ready = sem("xT_lo_ready")
        dve_step = sem("dve_step")
        in0_ready = sem("in0_ready")
        v_gelu = sem("v_gelu")
        v_var_ready = sem("v_var_ready")
        v_rs_ready = sem("v_rs_ready")
        v_normed = sem("v_normed")
        v_hi_ready = sem("v_hi_ready")
        v_lo_ready = sem("v_lo_ready")
        mixed_ready = sem("mixed_ready")
        mixed_kept = sem("mixed_kept")
        a_hi_ready = sem("a_hi_ready")
        a_lo_ready = sem("a_lo_ready")
        pooled_ready = sem("pooled_ready")
        pd_hi_ready = sem("pd_hi_ready")
        pd_lo_ready = sem("pd_lo_ready")
        group_ready = sem("group_ready")
        ga_hi_ready = sem("ga_hi_ready")
        ga_lo_ready = sem("ga_lo_ready")
        u_scaled = sem("u_scaled")
        u_gelu = sem("u_gelu")
        gated_ready = sem("gated_ready")
        gb_hi_ready = sem("gb_hi_ready")
        gb_lo_ready = sem("gb_lo_ready")
        gu0_ready = sem("gu0_ready")
        silu_ready = sem("silu_ready")
        hid_ready = sem("hid_ready")
        hid_turned = sem("hid_turned")
        hT_hi_ready = sem("hT_hi_ready")
        hT_lo_ready = sem("hT_lo_ready")
        glu_ready = sem("glu_ready")
        tap_done = sem("tap_done")
        taps_copied = sem("taps_copied")
        conv_ready = sem("conv_ready")
        gate_ready = sem("gate_ready")
        conv_last_ready = sem("conv_last_ready")
        prod_ready = sem("prod_ready")
        prod_used = sem("prod_used")
        cst_diag_ready = sem("cst_diag_ready")
        cst_spread = sem("cst_spread")
        sq_ready = sem("sq_ready")
        sq_added = sem("sq_added")
        sq_summed = sem("sq_summed")
        glu_tail_ready = sem("glu_tail_ready")
        cvar_ready = sem("cvar_ready")
        crs_ready = sem("crs_ready")
        c_centred = sem("c_centred")
        c_normed = sem("c_normed")
        c_silu = sem("c_silu")
        cT_hi_ready = sem("cT_hi_ready")
        cT_lo_ready = sem("cT_lo_ready")

        def y_bank(par, t, c):
            return 4 * (par if c >= 2 else 1 - par) + 2 * t + c % 2

        def turn_bank(b, par, t, c):
            return y_bank(par, t, c) if b else 4 + 2 * t + c % 2

        def wait_sum(eng, t, ready0, count0, q):
            if t == 0:
                eng.wait_ge(ready0, count0)
            else:
                eng.wait_ge(units_used, used_count(q, 3))

        def wait_y(eng, e, j, t):
            wait_sum(eng, t, y0_ready, 2 * e + j + 1, Y_LAST[e][j])

        def pairs(bank):
            return acc[:, bank, :].rearrange("p (k n) -> p k n", n=P)

        block = ctx.enter_context(nc.Block())

        @block.sync
        def _(sp):
            def load(q, s):
                sp.dma_start(raw[:, s, :], d_units[q * 4 + s]).then_inc(raw_landed[s], 16)

            def load_x(t, h):
                hs = slice(h * UNIT, (h + 1) * UNIT)
                sp.dma_start(x[:, t, hs], d_x[t * P:(t + 1) * P, hs]).then_inc(x_landed[t][h], 16)

            sp.dma_start(ident[:], d_ident).then_inc(ident_landed, 16)
            load_x(0, 0)
            load(0, 0)
            sp.dma_start(vecs[:], d_vecs).then_inc(vecs_landed, 16)
            load_x(1, 0)
            for s in range(1, 4):
                load(0, s)
            load_x(0, 1)
            load_x(1, 1)
            with sp.Fori(1, Q_POOL0 + 1) as q:
                for s in range(4):
                    sp.wait_ge(lo_ready, lo_count(q - 1, s))
                    load(q, s)
            with sp.Fori(Q_POOL0 + 1, Q_POOL1 + 1) as q:
                for s in range(4):
                    sp.wait_ge(lo_ready_pool, lo_pool_count(q - 1, s))
                    load(q, s)
            with sp.Fori(Q_POOL1 + 1, Q_END) as q:
                for s in range(4):
                    sp.wait_ge(lo_ready, lo_count(q - 1, s, True))
                    load(q, s)
            for t in range(T):
                for c in range(4):
                    cs = slice(c * BANK, (c + 1) * BANK)
                    sp.wait_ge(x_ready, added(4, t, c))
                    sp.dma_start(d_out[t * P:(t + 1) * P, cs], x[:, t, cs]).then_inc(out_stored, 16)
            sp.wait_ge(out_stored, 16 * 4 * T)

        @block.gpsimd
        def _(pool):
            def inv_root(ready, count, out, var, done):
                pool.wait_ge(ready, count)
                nc.gpsimd.tensor_tensor(out, var, pow_exp[:].to_broadcast([P, out.shape[-1]]), ALU.pow).then_inc(done, 1)

            def load_post(e):
                if e:
                    pool.wait_ge(y_gained, 8 * e)
                pool.dma_start(gpost[:], d_post[e:e + 1, :].to_broadcast([P, D])).then_inc(post_landed, 16)

            def norm_in(b):
                for t in range(T):
                    inv_root(x_var_ready, 2 * b + t + 1, x_rs[:, t:t + 1], x_var[:, t, 1:2], x_rs_ready)

            def split(q, s):
                pool.wait_ge(hi_ready, hi_count(q, s))
                nc.gpsimd.tensor_tensor(w_lo[:, s, :], raw[:, s, :], w_hi[:, s, :],
                                        ALU.subtract).then_inc(lo_ready_pool, 1)

            def norm_out(e):
                y = [(y_var_ready, 2 * e + t + 1, y_rs[:, t:t + 1], y_var[:, t, 1:2], y_rs_ready) for t in range(T)]
                x_ = [(x_var_ready, 2 * e + t + 3, x_rs[:, t:t + 1], x_var[:, t, 1:2], x_rs_ready) for t in range(T)]
                if e == 1:
                    inv_root(*y[0])
                    split(Q_PW1, 0)
                    inv_root(*x_[0])
                    inv_root(*y[1])
                    split(Q_PW1, 1)
                    inv_root(*x_[1])
                    split(Q_PW1, 2)
                    split(Q_PW1, 3)
                else:
                    for root in y if e == 3 else y + x_:
                        inv_root(*root)

            nc.gpsimd.memset(pow_exp[:], -0.5).then_inc(consts_set, 1)
            nc.gpsimd.memset(ones[:], 1.0).then_inc(consts_set, 1)
            pool.wait_ge(consts_set, 1)
            norm_in(0)
            load_post(0)
            pool.dma_start(bs[:], d_bs[0:1].to_broadcast([P, HEADS, P])).then_inc(bs_landed, 16)
            pool.wait_ge(raw_landed[3], 16 * (Q_CONST + 1))
            w_s = raw[:, 3, BANK:].rearrange("p (h n) -> p h n", h=HEADS)
            nc.gpsimd.affine_select(out=w_s, in_=w_s, compare_op=ALU.is_ge, fill=0.0, base=0,
                                    pattern=[[0, HEADS], [1, P]], channel_multiplier=-1).then_inc(w_s_masked, 1)
            pool.wait_ge(rs_spread, 1)
            pool.dma_start(tok[:, 0:DA], d_lng[0:1, :].to_broadcast([P, DA])).then_inc(lngb_landed, 16)
            pool.dma_start(tok[:, DA:D], d_lnb[0:1, :].to_broadcast([P, DA])).then_inc(lngb_landed, 16)
            for t in range(T):
                inv_root(v_var_ready, t + 1, ln_rs[:, t:t + 1], ln_var[:, t:t + 1], v_rs_ready)
            norm_out(0)
            load_post(1)
            norm_out(1)
            wait_y(pool, 1, 1, 1)
            nc.gpsimd.memset(g_now[:, :, 0:PAD], 0.0).then_inc(consts_set, 1)
            nc.gpsimd.memset(g_tail[:, :, :, 0:PAD], 0.0).then_inc(consts_set, 1)
            nc.gpsimd.memset(one_mean[:], 1.0 / D).then_inc(consts_set, 1)

            with pool.Fori(Q_PW1 + 1, Q_PW2) as q:
                for s in range(4):
                    split(q, s)
            pool.wait_ge(gate_ready, CCH)
            for par in (1, 0):
                for n in range(2):
                    nc.gpsimd.tensor_tensor(g_tail[:, par, n, PAD:], lin[:, par, n, :], sig[:, par, n, :],
                                            ALU.mult).then_inc(glu_tail_ready, 1)
            for c in range(1, SQ_POOL):
                pool.wait_ge(conv_ready, 2 * (c + 1))
                pool.wait_ge(sq_ready, c + 1)
                if c > 1:
                    pool.wait_ge(sq_added, 2 * (c - 1))
                first = (conv[:, 0:2, :], sq[:, 0]) if c == 1 else (conv_sum[:], sq_sum[:])
                nc.gpsimd.tensor_tensor(conv_sum[:], first[0], conv[:, 2 * c:2 * c + 2, :], ALU.add).then_inc(sq_added, 1)
                nc.gpsimd.tensor_tensor(sq_sum[:], first[1], sq[:, c % 2], ALU.add).then_inc(sq_added, 1)
            for s in range(4):
                split(Q_PW2, s)
            load_post(2)
            inv_root(cvar_ready, 1, crs[:], cvar[:, :, 1], crs_ready)
            norm_out(2)
            load_post(3)
            norm_out(3)

        @block.scalar
        def _(act):
            def split(q, s, gain=None, dst=None):
                act.wait_ge(raw_landed[s], (q + 1) * 16)
                if dst is None and not (isinstance(q, int) and q == 0):
                    act.wait_ge(units_used, used_count(q - (2 if isinstance(q, int) and q == Q_A else 1), s))
                out = w_hi[:, s, :] if dst is None else dst[:, s, :]
                scale = 1.0 if gain is None else vecs[:, gain:gain + 1]
                nc.scalar.activation(out, raw[:, s, :], ACT.Copy, scale=scale).then_inc(hi_ready, 1)

            def split_quad(q, gain=None, k0=0):
                for s in range(4):
                    split(q, s, None if gain is None else gain + k0 + s)

            def square(n, src, total):
                if n >= 2:
                    act.wait_ge(squared, n - 1)
                nc.scalar.activation(junk[:, n % 2, :], src, ACT.Square, accum_out=total).then_inc(squared, 1)

            def square_y(e, par, t, cs):
                for c in cs:
                    j = c // 2
                    if c == 2:
                        act.wait_ge(y2_ready, 2 * e + t + 1)
                    else:
                        wait_y(act, e, j, t)
                    square(y_square(e, t, c), acc[:, y_bank(par, t, c), :], y_sums[:, t, c:c + 1])

            def square_x(b, t, cs):
                for c in cs:
                    if b:
                        act.wait_ge(x_ready, added(b, t, c))
                    else:
                        act.wait_ge(x_landed[t][c // 2], 16)
                    square(x_square(b, t, c), x[:, t, c * BANK:(c + 1) * BANK], x_sums[:, t, c:c + 1])

            def hi_xT(b, par, t, cs, gain=None):
                for c in cs:
                    act.wait_ge(x_turned, turned(b, t, c))
                    src = pairs(turn_bank(b, par, t, c))
                    dst = xT_hi[:, 4 * c:4 * c + 4, t * P:(t + 1) * P]
                    if gain is None:
                        nc.scalar.activation(dst, src, ACT.Copy).then_inc(xT_hi_ready, 1)
                    else:
                        for n in range(4):
                            g = gain + 4 * c + n
                            last = nc.scalar.activation(dst[:, n, :], src[:, n, :], ACT.Copy, scale=vecs[:, g:g + 1])
                        last.then_inc(xT_hi_ready, 1)

            def open_ffn(e, par, q, gain):
                b = e + 1
                square_y(e, par, 0, (2, 3))
                split(q, 0, gain)
                split(q, 1, gain + 1)
                hi_xT(b, par, 0, (0, 1))
                square_y(e, par, 1, (2, 3))
                split(q, 2, gain + 2)
                split(q, 3, gain + 3)
                hi_xT(b, par, 1, (0, 1))
                split_quad(q + 1, gain, 4)
                split(q + 2, 0, gain + 8)
                hi_xT(b, par, 0, (2, 3))
                split(q + 2, 1, gain + 9)
                hi_xT(b, par, 1, (2, 3))
                split(q + 2, 2, gain + 10)
                split(q + 2, 3, gain + 11)
                square_x(b, 0, range(4))
                square_x(b, 1, range(4))
                split_quad(q + 3, gain, 12)

            ab = V_PRE["ab"]
            act.wait_ge(consts_set, 1)
            nc.scalar.activation(warm[:], pow_exp[:], ACT.Square)
            hi_xT(0, 1, 0, (0,))
            act.wait_ge(vecs_landed, 16)
            split(Q_V, 0, ab)
            hi_xT(0, 1, 1, (0,))
            for s in range(1, 4):
                split(Q_V, s, ab + s)
            split(Q_V + 1, 0, ab + 4)
            for c in range(1, 4):
                for t in range(T):
                    hi_xT(0, 1, t, (c,))
                split(Q_V + 1, c, ab + 4 + c)
            for s in range(4):
                split(Q_V + 2, s, ab + 8 + s)
                square_x(0, s // 2, (2 * (s % 2), 2 * (s % 2) + 1))
            split_quad(Q_V + 3, ab, 12)
            for s in range(4):
                if s == 3:
                    act.wait_ge(w_s_masked, 1)
                split(Q_CONST, s, dst=c_hi)
            split_quad(Q_A, ab, 0)
            act.wait_ge(x_rs_ready, 2)
            for t in range(T):
                wait_sum(act, t, in0_ready, 1, Q_V + 3)
                for h in range(2):
                    nc.scalar.activation(vm[:, t * DA + h * BANK:t * DA + (h + 1) * BANK], acc[:, 2 * t + h, :],
                                         ACT.Gelu_apprx_tanh, scale=x_rs[:, t:t + 1]).then_inc(v_gelu, 1)
            split_quad(Q_A + 1, ab, 4)
            for t in range(T):
                split(Q_A + 2, 2 * t, ab + 8 + 2 * t)
                act.wait_ge(v_normed, t + 1)
                nc.scalar.activation(vd_hi[:, t * DA:(t + 1) * DA], vm[:, t * DA:(t + 1) * DA],
                                     ACT.Copy).then_inc(v_hi_ready, 1)
                split(Q_A + 2, 2 * t + 1, ab + 9 + 2 * t)
            split_quad(Q_A + 3, ab, 12)
            split_quad(Q_U, ab, 0)
            for t in range(T):
                wait_sum(act, t, in0_ready, 2, Q_A + 3)
                for h in range(2):
                    n = t * 4 + h * 2
                    nc.scalar.activation(mix_hi[:, 8 + n:10 + n, :], acc[:, 4 + 2 * t + h, :].rearrange(
                        "p (k n) -> p k n", n=SEQ), ACT.Copy, scale=x_rs[:, t:t + 1]).then_inc(a_hi_ready, 1)
            split_quad(Q_U + 1, ab, 4)
            for g in range(4):
                act.wait_ge(pooled_ready, g + 1)
                nc.scalar.activation(vd_hi[:, g * BANK:(g + 1) * BANK], acc[:, 4 + g, :], ACT.Copy).then_inc(pd_hi_ready, 1)
            split_quad(Q_U + 2, ab, 8)
            for g in range(4):
                act.wait_ge(group_ready, g + 1)
                for n in range(2):
                    k = 2 * g + n
                    last = nc.scalar.activation(mix_hi[:, k, :], acc[:, 4 + g, n * SEQ:(n + 1) * SEQ], ACT.Copy,
                                                scale=vecs[:, V_ASCALE + k:V_ASCALE + k + 1])
                last.then_inc(ga_hi_ready, 1)
            split_quad(Q_U + 3, ab, 12)
            split_quad(Q_OUT)
            for g in range(4):
                act.wait_ge(u_scaled, g + 1)
                nc.scalar.activation(acc[:, g, :], acc[:, g, :], ACT.Gelu_apprx_tanh).then_inc(u_gelu, 1)
            for g in range(4):
                act.wait_ge(gated_ready, g + 1)
                nc.scalar.activation(mix_hi[:, 8 + 2 * g:10 + 2 * g, :], vm[:, g * BANK:(g + 1) * BANK].rearrange(
                    "p (k n) -> p k n", n=SEQ), ACT.Copy).then_inc(gb_hi_ready, 1)
                split(Q_OUT + 1, g)
            split_quad(Q_OUT + 2)
            split_quad(Q_OUT + 3)
            split_quad(Q_OUT + 4)
            square_y(0, 0, 0, (0, 1))
            square_y(0, 0, 1, (0, 1))
            for k in range(5, 8):
                split_quad(Q_OUT + k)
            open_ffn(0, 0, Q_F0, V_PRE["f0"])

            def ffn(layer, q0, gain, par, e):
                act.wait_ge(x_rs_ready, 2 * (e - 1) + 4)

                def silu(i, bank_par, t):
                    wait_sum(act, t, gu0_ready, i + (11 * layer + 1), i * 4 + (q0 + 3))
                    nc.scalar.activation(tok[:, t * DA + BANK:(t + 1) * DA], acc[:, 4 * bank_par + 2 * t, :],
                                         ACT.Silu, scale=x_rs[:, t:t + 1]).then_inc(silu_ready, 1)

                def hi_hid(i, bank_par, t):
                    act.wait_ge(hid_turned, i * 2 + (22 * layer + t + 1))
                    nc.scalar.activation(hT_hi[:, bass.ts(i, 4), t * P:(t + 1) * P], pairs(4 * bank_par + 2 * t),
                                         ACT.Copy).then_inc(hT_hi_ready, 1)

                def chunk(i, bank_par):
                    split_quad(i * 4 + q0, gain, 0)
                    silu(i - 1, bank_par, 0)
                    silu(i - 1, bank_par, 1)
                    split_quad(i * 4 + (q0 + 1), gain, 4)
                    hi_hid(i - 1, bank_par, 0)
                    hi_hid(i - 1, bank_par, 1)
                    split_quad(i * 4 + (q0 + 2), gain, 8)
                    split_quad(i * 4 + (q0 + 3), gain, 12)

                with act.Fori(0, (FFC - 1) // 2) as n:
                    chunk(n * 2 + 1, par)
                    chunk(n * 2 + 2, 1 - par)
                qd = q0 + Q_FF
                split_quad(qd)
                silu(FFC - 1, par, 0)
                silu(FFC - 1, par, 1)
                split_quad(qd + 1)
                hi_hid(FFC - 1, par, 0)
                hi_hid(FFC - 1, par, 1)
                with act.Fori(qd + 2, qd + Q_DOWN // 2 + 1) as q:
                    split_quad(q)
                square_y(e, par, 0, (0, 1))
                square_y(e, par, 1, (0, 1))
                with act.Fori(qd + Q_DOWN // 2 + 1, qd + Q_DOWN) as q:
                    split_quad(q)

            ffn(0, Q_F0, V_PRE["f0"], 1, 1)
            c_gain = V_PRE["c"]
            square_y(1, 1, 0, (2, 3))
            split(Q_PW1, 0)
            square_x(2, 0, range(4))
            square_y(1, 1, 1, (2, 3))
            split(Q_PW1, 1)
            square_x(2, 1, range(4))
            hi_xT(2, 1, 0, (0, 1), c_gain)
            hi_xT(2, 1, 1, (0, 1), c_gain)
            split(Q_PW1, 2)
            split(Q_PW1, 3)
            hi_xT(2, 1, 0, (2, 3), c_gain)
            hi_xT(2, 1, 1, (2, 3), c_gain)

            act.wait_ge(x_turned, 24)
            act.dma_start(taps[:], d_taps).then_inc(taps_landed, 16)
            for row in (0, 32):
                act.dma_start(tok[row:row + 1, :], d_bpw2[0:1, :]).then_inc(bpw2_landed, 16)

            def split_bias():
                act.wait_ge(bpw2_landed, 32)
                act.wait_ge(bias_cleared, 1)
                for row in (0, 32):
                    nc.scalar.activation(bias_rows[row:row + 1, :], tok[row:row + 1, :], ACT.Copy).then_inc(bias_hi_ready, 1)
                act.wait_ge(consts_set, 2)
                nc.scalar.activation(ones_r[:], ones[0:64, :], ACT.Copy).then_inc(bias_hi_ready, 1)

            def gate(c, par):
                split_quad(c * 2 + (Q_PW1 + 1))
                if isinstance(c, int) and c == 0:
                    split_bias()
                last_chunk = isinstance(c, int) and c == CCH - 1
                for s in range(3 if last_chunk else 4):
                    split(c * 2 + (Q_PW1 + 2), s)
                if isinstance(c, int) and c == 0:
                    act.wait_ge(consts_set, 1)
                    nc.scalar.activation(warm[:], pow_exp[:], ACT.Sigmoid)
                act.wait_ge(units_used, used_count(c * 2 + (Q_PW1 + 1), 3))
                if not isinstance(c, int) or c >= 2:
                    act.wait_ge(glu_ready, c * 2 - 2)
                for n in range(2):
                    k = c * 2 + n
                    nc.scalar.activation(sig[:, par, n, :], acc[:, 4 * par + n, SEQ:2 * SEQ], ACT.Sigmoid,
                                         bias=vecs[:, bass.ds(V_BG + k, 1)])
                    last = nc.scalar.activation(lin[:, par, n, :], acc[:, 4 * par + n, 0:SEQ], ACT.Identity,
                                                bias=vecs[:, bass.ds(V_BA + k, 1)])
                last.then_inc(gate_ready, 1)

            gate(0, 0)
            gate(1, 1)
            with act.Fori(1, CCH // 2 - 1) as n:
                gate(n * 2, 0)
                gate(n * 2 + 1, 1)
            gate(CCH - 2, 0)
            gate(CCH - 1, 1)

            def square_conv(place, c):
                if c == CCH - 1:
                    act.wait_ge(conv_last_ready, 2)
                else:
                    act.wait_ge(conv_ready, 2 * (c + 1))
                if 2 <= place < SQ_POOL + 2:
                    act.wait_ge(sq_added, 2 * max(place - 2, 1))
                nc.scalar.activation(sq[:, place % 2], conv[:, 2 * c:2 * c + 2, :], ACT.Square).then_inc(sq_ready, 1)

            def hi_c(k):
                act.wait_ge(c_silu, k + 1)
                nc.scalar.activation(cT_hi[:, k, :], conv[:, k, :], ACT.Copy).then_inc(cT_hi_ready, 1)

            square_conv(0, 0)
            square_conv(1, 1)
            act.wait_ge(taps_landed, 16)
            act.wait_ge(glu_tail_ready, 2)
            for j in range(TAPS):
                for n in range(2):
                    i = 2 * j + n
                    if i >= 4:
                        act.wait_ge(prod_used, i - 3)
                    k = 2 * (CCH - 1) + n
                    nc.scalar.activation(prod[:, i % 4, :], g_tail[:, 1, n, j:j + SEQ], ACT.Copy,
                                         scale=taps[:, k, j:j + 1]).then_inc(prod_ready, 1)
                if j % 3 == 2 and 2 + j // 3 < SQ_POOL:
                    square_conv(2 + j // 3, 2 + j // 3)
                if j == 3 * SQ_POOL - 6:
                    split(Q_PW2, 3)
            act.wait_ge(prod_used, 2 * TAPS)
            for n in range(2):
                k = 2 * (CCH - 1) + n
                nc.scalar.activation(conv[:, k, :], acc[:, 4, n * SEQ:(n + 1) * SEQ], ACT.Identity,
                                     bias=vecs[:, V_BDW + k:V_BDW + k + 1]).then_inc(conv_last_ready, 1)
            square_conv(6, SQ_ORDER[6])
            square_conv(7, SQ_ORDER[7])
            for k in range(KT):
                act.wait_ge(c_normed, k + 1)
                nc.scalar.activation(conv[:, k, :], conv[:, k, :], ACT.Silu, bias=vecs[:, V_LNB + k:V_LNB + k + 1],
                                     scale=vecs[:, V_LNG + k:V_LNG + k + 1]).then_inc(c_silu, 1)
                if k:
                    hi_c(k - 1)
                if k >= KT // 2 and k % 2:
                    split(Q_PW2 + 1, k // 2 - KT // 4)
            hi_c(KT - 1)
            for k in range(2, 5):
                split_quad(Q_PW2 + k)
            square_y(2, 1, 0, (0, 1))
            square_y(2, 1, 1, (0, 1))
            for k in range(5, 8):
                split_quad(Q_PW2 + k)
            open_ffn(2, 1, Q_F1, V_PRE["f1"])
            ffn(1, Q_F1, V_PRE["f1"], 0, 3)
            square_y(3, 0, 0, (2, 3))
            square_y(3, 0, 1, (2, 3))

        @block.vector
        def _(dve):
            steps = [0]

            def after(ins):
                steps[0] += 1
                ins.then_inc(dve_step, 1)
                dve.wait_ge(dve_step, steps[0])

            def split(q, s, gain=None, dst=None):
                dve.wait_ge(hi_ready, hi_count(q, s))
                out, hi = (w_lo, w_hi) if dst is None else dst
                if gain is None:
                    ins = nc.vector.tensor_tensor(out[:, s, :], raw[:, s, :], hi[:, s, :], ALU.subtract)
                else:
                    ins = nc.vector.scalar_tensor_tensor(out[:, s, :], raw[:, s, :], vecs[:, gain:gain + 1], hi[:, s, :],
                                                         ALU.mult, ALU.subtract)
                ins.then_inc(lo_ready, 1)

            def split_quad(q, gain=None, k0=0):
                for s in range(4):
                    split(q, s, None if gain is None else gain + k0 + s)

            def gain_y(e, par, t, cs):
                dve.wait_ge(post_landed, 16 * (e + 1))
                for c in cs:
                    dve.wait_ge(squared, y_square(e, t, c) + 1)
                    b = y_bank(par, t, c)
                    nc.vector.tensor_tensor(acc[:, b, :], acc[:, b, :], gpost[:, c * BANK:(c + 1) * BANK],
                                            ALU.mult).then_inc(y_gained, 1)

            def mean_square(sums, var, t, count, ready):
                dve.wait_ge(squared, count)
                after(nc.vector.reduce_sum(var[:, t, 0:1], sums[:, t, :], axis=AX.X))
                nc.vector.tensor_scalar(var[:, t, 1:2], var[:, t, 0:1], 1.0 / D, EPS, ALU.mult, ALU.add).then_inc(ready, 1)

            def spread_rs(b, t):
                dve.wait_ge(x_rs_ready, 2 * b + t + 1)
                nc.vector.tensor_scalar(rs_diag[:, t, :], ident[:], x_rs[:, t:t + 1], None, ALU.mult).then_inc(rs_diag_ready, 1)

            def add_y(e, par, t, cs):
                for c in cs:
                    dve.wait_ge(y_rs_ready, 2 * e + t + 1)
                    dve.wait_ge(y_gained, 8 * e + (2 * t + c if c < 2 else 2 + 2 * t + c) + 1)
                    xs = x[:, t, c * BANK:(c + 1) * BANK]
                    nc.vector.scalar_tensor_tensor(xs, acc[:, y_bank(par, t, c), :], y_rs[:, t:t + 1], xs,
                                                   ALU.mult, ALU.add).then_inc(x_ready, 1)

            def lo_xT(b, par, t, cs, gain=None):
                for c in cs:
                    dve.wait_ge(xT_hi_ready, parted(b, t, c))
                    src = pairs(turn_bank(b, par, t, c))
                    hi = xT_hi[:, 4 * c:4 * c + 4, t * P:(t + 1) * P]
                    dst = xT_lo[:, 4 * c:4 * c + 4, t * P:(t + 1) * P]
                    if gain is None:
                        nc.vector.tensor_tensor(dst, src, hi, ALU.subtract).then_inc(xT_lo_ready, 1)
                    else:
                        for n in range(4):
                            g = gain + 4 * c + n
                            last = nc.vector.scalar_tensor_tensor(dst[:, n, :], src[:, n, :], vecs[:, g:g + 1], hi[:, n, :],
                                                                  ALU.mult, ALU.subtract)
                        last.then_inc(xT_lo_ready, 1)

            def open_ffn(e, par, q, gain):
                b = e + 1
                mean_square(y_sums, y_var, 0, y_square(e, 0, 3) + 1, y_var_ready)
                add_y(e, par, 0, (0, 1))
                split(q, 0, gain)
                lo_xT(b, par, 0, (0, 1))
                split(q, 1, gain + 1)
                mean_square(y_sums, y_var, 1, y_square(e, 1, 3) + 1, y_var_ready)
                split(q, 2, gain + 2)
                add_y(e, par, 1, (0, 1))
                split(q, 3, gain + 3)
                lo_xT(b, par, 1, (0, 1))
                gain_y(e, par, 0, (2, 3))
                split(q + 1, 0, gain + 4)
                add_y(e, par, 0, (2, 3))
                split(q + 1, 1, gain + 5)
                gain_y(e, par, 1, (2, 3))
                split(q + 1, 2, gain + 6)
                add_y(e, par, 1, (2, 3))
                split(q + 1, 3, gain + 7)
                split(q + 2, 0, gain + 8)
                lo_xT(b, par, 0, (2, 3))
                split(q + 2, 1, gain + 9)
                lo_xT(b, par, 1, (2, 3))
                split(q + 2, 2, gain + 10)
                split(q + 2, 3, gain + 11)
                for t in range(T):
                    mean_square(x_sums, x_var, t, x_square(b, t, 3) + 1, x_var_ready)
                split_quad(q + 3, gain, 12)

            ab = V_PRE["ab"]
            lo_xT(0, 1, 0, (0,))
            dve.wait_ge(vecs_landed, 16)
            split(Q_V, 0, ab)
            lo_xT(0, 1, 1, (0,))
            for s in range(1, 4):
                split(Q_V, s, ab + s)
            split(Q_V + 1, 0, ab + 4)
            for c in range(1, 4):
                for t in range(T):
                    lo_xT(0, 1, t, (c,))
                split(Q_V + 1, c, ab + 4 + c)
            split_quad(Q_V + 2, ab, 8)
            for t in range(T):
                mean_square(x_sums, x_var, t, x_square(0, t, 3) + 1, x_var_ready)
            dve.wait_ge(ident_landed, 16)
            for t in range(T):
                spread_rs(0, t)
            split_quad(Q_V + 3, ab, 12)
            dve.wait_ge(rs_spread, 1)
            nc.vector.tensor_copy(rs_row[:], acc[:, 4:5, 0:SEQ]).then_inc(rs_row_ready, 1)
            for s in range(4):
                split(Q_CONST, s, dst=(c_lo, c_hi))
            split_quad(Q_A, ab, 0)
            for t in range(T):
                for h in range(2):
                    dve.wait_ge(v_gelu, 2 * t + h + 1)
                    last = nc.vector.bn_stats(bn[:, t, 6 * h:6 * h + 6], vm[:, t * DA + h * BANK:t * DA + (h + 1) * BANK])
                after(last)
                after(nc.vector.bn_aggr(mv[:, t, :], bn[:, t, :]))
                nc.vector.tensor_scalar(ln_var[:, t:t + 1], mv[:, t, 1:2], EPS, None, ALU.add).then_inc(v_var_ready, 1)
                split(Q_A + 1, t, ab + 4 + t)
            for t in range(T):
                dve.wait_ge(v_rs_ready, t + 1)
                vt = vm[:, t * DA:(t + 1) * DA]
                after(nc.vector.tensor_scalar(vt, vt, mv[:, t, 0:1], ln_rs[:, t:t + 1], ALU.subtract, ALU.mult))
                if t == 0:
                    split(Q_A + 1, 2, ab + 6)
                else:
                    split(Q_A + 2, 0, ab + 8)
                dve.wait_ge(lngb_landed, 32)
                after(nc.vector.tensor_tensor(vt, vt, tok[:, 0:DA], ALU.mult))
                nc.vector.tensor_tensor(vt, vt, tok[:, DA:D], ALU.add).then_inc(v_normed, 1)
                if t == 0:
                    split(Q_A + 1, 3, ab + 7)
            split(Q_A + 2, 1, ab + 9)
            for t in range(T):
                dve.wait_ge(v_hi_ready, t + 1)
                dve.wait_ge(v_normed, t + 1)
                nc.vector.tensor_tensor(vd_lo[:, t * DA:(t + 1) * DA], vm[:, t * DA:(t + 1) * DA],
                                        vd_hi[:, t * DA:(t + 1) * DA], ALU.subtract).then_inc(v_lo_ready, 1)
                split(Q_A + 2, 2 + t, ab + 10 + t)
            dve.wait_ge(bs_landed, 16)
            dve.wait_ge(v_lo_ready, 2)
            split_quad(Q_A + 3, ab, 12)
            for h in range(HEADS):
                dve.wait_ge(mixed_ready, h + 1)
                nc.vector.tensor_tensor(vm[:, h * BANK:(h + 1) * BANK].rearrange("p (k n) -> p k n", n=P), pairs(h),
                                        bs[:, h:h + 1, :].to_broadcast([P, 4, P]), ALU.add).then_inc(mixed_kept, 1)
            split_quad(Q_U, ab, 0)
            for t in range(T):
                for h in range(2):
                    n = t * 4 + h * 2
                    dve.wait_ge(a_hi_ready, 2 * t + h + 1)
                    nc.vector.scalar_tensor_tensor(mix_lo[:, 8 + n:10 + n, :], acc[:, 4 + 2 * t + h, :].rearrange(
                        "p (k n) -> p k n", n=SEQ), x_rs[:, t:t + 1], mix_hi[:, 8 + n:10 + n, :],
                        ALU.mult, ALU.subtract).then_inc(a_lo_ready, 1)
            split_quad(Q_U + 1, ab, 4)
            for g in range(4):
                dve.wait_ge(pd_hi_ready, g + 1)
                nc.vector.tensor_tensor(vd_lo[:, g * BANK:(g + 1) * BANK], acc[:, 4 + g, :],
                                        vd_hi[:, g * BANK:(g + 1) * BANK], ALU.subtract).then_inc(pd_lo_ready, 1)
            split_quad(Q_U + 2, ab, 8)
            for g in range(4):
                dve.wait_ge(ga_hi_ready, g + 1)
                for n in range(2):
                    k = 2 * g + n
                    last = nc.vector.scalar_tensor_tensor(mix_lo[:, k, :], acc[:, 4 + g, n * SEQ:(n + 1) * SEQ],
                                                          vecs[:, V_ASCALE + k:V_ASCALE + k + 1], mix_hi[:, k, :],
                                                          ALU.mult, ALU.subtract)
                last.then_inc(ga_lo_ready, 1)
            split_quad(Q_U + 3, ab, 12)
            split_quad(Q_OUT)
            dve.wait_ge(rs_row_ready, 1)
            dve.wait_ge(units_used, used_count(Q_U + 3, 3))
            for g in range(4):
                u = acc[:, g, :].rearrange("p (k n) -> p k n", n=SEQ)
                nc.vector.tensor_tensor(u, u, rs_row[:].to_broadcast([P, 2, SEQ]), ALU.mult).then_inc(u_scaled, 1)
            dve.wait_ge(mixed_kept, HEADS)
            for g in range(4):
                dve.wait_ge(u_gelu, g + 1)
                nc.vector.tensor_tensor(vm[:, g * BANK:(g + 1) * BANK], acc[:, g, :], vm[:, g * BANK:(g + 1) * BANK],
                                        ALU.mult).then_inc(gated_ready, 1)
            for g in range(4):
                dve.wait_ge(gb_hi_ready, g + 1)
                nc.vector.tensor_tensor(mix_lo[:, 8 + 2 * g:10 + 2 * g, :], vm[:, g * BANK:(g + 1) * BANK].rearrange(
                    "p (k n) -> p k n", n=SEQ), mix_hi[:, 8 + 2 * g:10 + 2 * g, :], ALU.subtract).then_inc(gb_lo_ready, 1)
                split(Q_OUT + 1, g)
            for k in range(2, 5):
                split_quad(Q_OUT + k)
            gain_y(0, 0, 0, (0, 1))
            gain_y(0, 0, 1, (0, 1))
            for k in range(5, 8):
                split_quad(Q_OUT + k)
            open_ffn(0, 0, Q_F0, V_PRE["f0"])

            def ffn(layer, q0, gain, par, e):
                dve.wait_ge(x_rs_ready, 2 * (e - 1) + 4)

                def hidden(i, bank_par, t):
                    dve.wait_ge(silu_ready, i * 2 + (22 * layer + t + 1))
                    nc.vector.scalar_tensor_tensor(tok[:, t * DA:t * DA + BANK], acc[:, 4 * bank_par + 2 * t + 1, :],
                                                   x_rs[:, t:t + 1], tok[:, t * DA + BANK:(t + 1) * DA],
                                                   ALU.mult, ALU.mult).then_inc(hid_ready, 1)

                def lo_hid(i, bank_par, t):
                    dve.wait_ge(hT_hi_ready, i * 2 + (22 * layer + t + 1))
                    nc.vector.tensor_tensor(hT_lo[:, bass.ts(i, 4), t * P:(t + 1) * P], pairs(4 * bank_par + 2 * t),
                                            hT_hi[:, bass.ts(i, 4), t * P:(t + 1) * P], ALU.subtract).then_inc(hT_lo_ready, 1)

                def chunk(i, bank_par):
                    split_quad(i * 4 + q0, gain, 0)
                    hidden(i - 1, bank_par, 0)
                    hidden(i - 1, bank_par, 1)
                    split_quad(i * 4 + (q0 + 1), gain, 4)
                    lo_hid(i - 1, bank_par, 0)
                    lo_hid(i - 1, bank_par, 1)
                    split_quad(i * 4 + (q0 + 2), gain, 8)
                    split_quad(i * 4 + (q0 + 3), gain, 12)

                with dve.Fori(0, (FFC - 1) // 2) as n:
                    chunk(n * 2 + 1, par)
                    chunk(n * 2 + 2, 1 - par)
                qd = q0 + Q_FF
                split_quad(qd)
                hidden(FFC - 1, par, 0)
                hidden(FFC - 1, par, 1)
                split_quad(qd + 1)
                lo_hid(FFC - 1, par, 0)
                lo_hid(FFC - 1, par, 1)
                with dve.Fori(qd + 2, qd + Q_DOWN // 2 + 1) as q:
                    split_quad(q)
                gain_y(e, par, 0, (0, 1))
                gain_y(e, par, 1, (0, 1))
                with dve.Fori(qd + Q_DOWN // 2 + 1, qd + Q_DOWN) as q:
                    split_quad(q)

            ffn(0, Q_F0, V_PRE["f0"], 1, 1)
            c_gain = V_PRE["c"]
            gain_y(1, 1, 0, (2,))
            mean_square(y_sums, y_var, 0, y_square(1, 0, 3) + 1, y_var_ready)
            gain_y(1, 1, 0, (3,))
            add_y(1, 1, 0, range(4))
            mean_square(x_sums, x_var, 0, x_square(2, 0, 3) + 1, x_var_ready)
            mean_square(y_sums, y_var, 1, y_square(1, 1, 3) + 1, y_var_ready)
            gain_y(1, 1, 1, (2, 3))
            spread_rs(2, 0)
            add_y(1, 1, 1, range(4))
            mean_square(x_sums, x_var, 1, x_square(2, 1, 3) + 1, x_var_ready)
            spread_rs(2, 1)
            for cs in ((0, 1), (2, 3)):
                for t in range(T):
                    lo_xT(2, 1, t, cs, c_gain)

            nc.vector.memset(bias_rows[:].bitcast(F32), 0.0).then_inc(bias_cleared, 1)
            dve.wait_ge(bias_hi_ready, 3)
            nc.vector.tensor_tensor(bias_rows[32:33, :], tok[32:33, :], bias_rows[32:33, :],
                                    ALU.subtract).then_inc(bias_lo_ready, 1)

            dve.wait_ge(consts_set, 5)
            dve.wait_ge(taps_landed, 16)

            def glu(c, par):
                dve.wait_ge(gate_ready, c + 1)
                for n in range(2):
                    nc.vector.tensor_tensor(g_now[:, n, PAD:], lin[:, par, n, :], sig[:, par, n, :], ALU.mult).then_inc(glu_ready, 1)

            def convolve(c):
                tail = isinstance(c, int) and c == CCH - 2
                if not tail:
                    for n in range(2):
                        nc.vector.tensor_copy(taps_now[:, n, :], taps[:, bass.ds(c * 2 + n, 1), :].rearrange(
                            "p a n -> p (a n)")).then_inc(taps_copied, 1)
                    dve.wait_ge(taps_copied, c * 2 + 2)
                for j in range(TAPS):
                    for n in range(2):
                        m = acc[:, 7, n * SEQ:(n + 1) * SEQ]
                        src = g_tail[:, 0, n, j:j + SEQ] if tail else g_now[:, n, j:j + SEQ]
                        w = taps[:, 2 * c + n, j:j + 1] if tail else taps_now[:, n, j:j + 1]
                        if j == 0:
                            if tail:
                                dve.wait_ge(glu_tail_ready, 4)
                                dve.wait_ge(conv_ready, 2 * c)
                            else:
                                dve.wait_ge(glu_ready, c * 2 + (n + 1))
                            nc.vector.tensor_scalar(m, src, w, vecs[:, bass.ds(V_BDW + c * 2 + n, 1)],
                                                    ALU.mult, ALU.add).then_inc(tap_done, 1)
                            continue
                        dve.wait_ge(tap_done, c * (2 * (TAPS - 1)) + (2 * (j - 1) + n + 1))
                        if j < TAPS - 1:
                            nc.vector.scalar_tensor_tensor(m, src, w, m, ALU.mult, ALU.add).then_inc(tap_done, 1)
                        else:
                            nc.vector.scalar_tensor_tensor(conv[:, bass.ds(c * 2 + n, 1), :].rearrange("p a n -> p (a n)"),
                                                           src, w, m, ALU.mult, ALU.add).then_inc(conv_ready, 1)

            def chunk(c, par):
                if not isinstance(c, int) or c:
                    dve.wait_ge(conv_ready, c * 2)
                glu(c, par)
                convolve(c)

            def lo_c(k):
                dve.wait_ge(cT_hi_ready, k + 1)
                nc.vector.tensor_tensor(cT_lo[:, k, :], conv[:, k, :], cT_hi[:, k, :], ALU.subtract).then_inc(cT_lo_ready, 1)

            chunk(0, 0)
            chunk(1, 1)
            with dve.Fori(1, CCH // 2 - 1) as i:
                chunk(i * 2, 0)
                chunk(i * 2 + 1, 1)
            convolve(CCH - 2)
            dve.wait_ge(sq_summed, CCH - SQ_POOL + 1)
            after(nc.vector.tensor_copy(cst[:].rearrange("p t n -> p (t n)"), acc[:, 6, 0:2 * T]))
            after(nc.vector.tensor_tensor(cvar[:, :, 0], cst[:, :, 0], cst[:, :, 0], ALU.mult))
            after(nc.vector.tensor_tensor(cvar[:, :, 1], cst[:, :, 1], cvar[:, :, 0], ALU.subtract))
            nc.vector.tensor_scalar(cvar[:, :, 1], cvar[:, :, 1], 0.0, EPS, ALU.max, ALU.add).then_inc(cvar_ready, 1)
            for t in range(T):
                last = nc.vector.tensor_scalar(diag[:, 0, t * P:(t + 1) * P], ident[:], cst[:, t, 0:1], None, ALU.mult)
            last.then_inc(cst_diag_ready, 1)
            dve.wait_ge(crs_ready, 1)
            for t in range(T):
                last = nc.vector.tensor_scalar(diag[:, 1, t * P:(t + 1) * P], ident[:], crs[:, t:t + 1], None, ALU.mult)
            last.then_inc(cst_diag_ready, 1)

            def centre(k):
                nc.vector.tensor_tensor(conv[:, k, :], conv[:, k, :], acc[:, 7, 0:SEQ], ALU.subtract).then_inc(c_centred, 1)

            dve.wait_ge(cst_spread, 1)
            centre(0)
            centre(1)
            dve.wait_ge(cst_spread, 2)
            for k in range(KT):
                dve.wait_ge(c_centred, k + 1)
                nc.vector.tensor_tensor(conv[:, k, :], conv[:, k, :], acc[:, 6, 0:SEQ], ALU.mult).then_inc(c_normed, 1)
                if k < KT - 2:
                    centre(k + 2)
                if k > 1:
                    lo_c(k - 2)
                if k > KT // 2 and k % 2 == 0:
                    split(Q_PW2 + 1, k // 2 - KT // 4 - 1)
            lo_c(KT - 2)
            lo_c(KT - 1)
            split(Q_PW2 + 1, 3)
            for k in range(2, 5):
                split_quad(Q_PW2 + k)
            gain_y(2, 1, 0, (0, 1))
            gain_y(2, 1, 1, (0, 1))
            for k in range(5, 8):
                split_quad(Q_PW2 + k)
            open_ffn(2, 1, Q_F1, V_PRE["f1"])
            ffn(1, Q_F1, V_PRE["f1"], 0, 3)
            for t in range(T):
                gain_y(3, 0, t, (2,))
                mean_square(y_sums, y_var, t, y_square(3, t, 3) + 1, y_var_ready)
                gain_y(3, 0, t, (3,))
                add_y(3, 0, t, range(4))

        @block.tensor
        def _(pe):
            mm = nc.tensor.matmul

            def wait_split(q, s):
                if isinstance(q, int) and q >= Q_POOL1:
                    pe.wait_ge(lo_ready, lo_count(q, s, True))
                elif isinstance(q, int) and q >= Q_POOL0:
                    pe.wait_ge(lo_ready_pool, lo_pool_count(q, s))
                else:
                    pe.wait_ge(lo_ready, lo_count(q, s))

            def unit_by_token(s, lhs_hi, lhs_lo, k, par, t, start, stop, first_half_ready=None):
                xh, xl = lhs_hi[:, k, t * P:(t + 1) * P], lhs_lo[:, k, t * P:(t + 1) * P]
                passes = ((xh, w_hi), (xh, w_lo), (xl, w_hi))
                if first_half_ready is None:
                    order = [(xs, ws, h) for xs, ws in passes for h in range(2)]
                else:
                    order = [(xs, ws, h) for h in range(2) for xs, ws in passes]
                for n, (xs, ws, h) in enumerate(order):
                    last = mm(acc[:, 4 * par + 2 * t + h, :], xs, ws[:, s, h * BANK:(h + 1) * BANK],
                              start=start and ws is w_hi and xs is xh, stop=stop and xs is xl)
                    if first_half_ready is not None and n == 2:
                        last.then_inc(first_half_ready, 1)
                return last

            def block_by_channel(s, col, k, bank, half, start, stop):
                out = acc[:, bank, half * SEQ:(half + 1) * SEQ]
                wh, wl = w_hi[:, s, col:col + P], w_lo[:, s, col:col + P]
                mm(out, wh, xT_hi[:, k, :], start=start and half == 0, stop=False, skip_group_check=True)
                mm(out, wh, xT_lo[:, k, :], start=False, stop=False, skip_group_check=True)
                return mm(out, wl, xT_hi[:, k, :], start=False, stop=stop, skip_group_check=True)

            def quad(q, lhs_hi, lhs_lo, k0, par, start=False, stop=None, before=None, after_pool=False, by_tile=False):
                order = [(t, s) for t in range(T) for s in range(4)] if by_tile else [(t, s) for s in range(4) for t in range(T)]
                for t, s in order:
                    if before is not None:
                        before(t, s)
                    if t == 0:
                        if after_pool:
                            pe.wait_ge(lo_ready, lo_count(q, s, True))
                        else:
                            wait_split(q, s)
                    last = unit_by_token(s, lhs_hi, lhs_lo, k0 + s, par, t, start and s == 0, stop is not None and s == 3,
                                         y2_ready if by_tile and s == 3 else None)
                    if t == T - 1:
                        last.then_inc(units_used, 1)
                    elif stop is not None and s == 3:
                        last.then_inc(stop, 1)

            def turn_x(b, par, t, cs):
                for c in cs:
                    if b == 0:
                        pe.wait_ge(x_landed[t][c // 2], 16)
                        if c >= 2:
                            pe.wait_ge(xT_lo_ready, parted(0, t, c - 2))
                    elif b == 2:
                        pe.wait_ge(rs_diag_ready, T + t + 1)
                    else:
                        pe.wait_ge(x_ready, added(b, t, c))
                    for n in range(4):
                        k = 4 * c + n
                        src, dst = x[:, t, k * P:(k + 1) * P], pairs(turn_bank(b, par, t, c))[:, n, :]
                        if b == 2:
                            last = mm(dst, src, rs_diag[:, t, :], start=n == 0, stop=n == 3, skip_group_check=True)
                        else:
                            last = nc.tensor.transpose(dst, src, ident[:])
                    last.then_inc(x_turned, 1)

            def turn_first(b, y_par):
                def before(t, s):
                    if t == 1 and s == 3:
                        turn_x(b, y_par, 0, (0, 1))
                return before

            def open_ffn(q, b, y_par, par, after_pool):
                for t in range(T):
                    for s in range(4):
                        if t == 0 and s == 3:
                            turn_x(b, y_par, 1, (0, 1))
                        if t == 0:
                            if after_pool:
                                pe.wait_ge(lo_ready, lo_count(q, s, True))
                            else:
                                wait_split(q, s)
                        if s == 0:
                            pe.wait_ge(xT_lo_ready, parted(b, t, 1))
                        last = unit_by_token(s, xT_hi, xT_lo, s, par, t, s == 0, False)
                        if t == T - 1:
                            last.then_inc(units_used, 1)

            def x_quads(q, b, y_par, par, stop, after_pool=False):
                for c in range(1, 4):
                    pe.wait_ge(xT_lo_ready, parted(b, 1, c))

                    def turn_rest(t, s):
                        if t == 0 and s >= 2:
                            turn_x(b, y_par, s - 2, (2, 3))

                    quad(q + c, xT_hi, xT_lo, 4 * c, par, stop=stop if c == 3 else None, after_pool=after_pool,
                         before=turn_rest if c == 1 and b % 2 else None)

            def turn_next(q):
                def before(t, s):
                    c = {(0, 3): 1, (1, 0): 2, (1, 2): 3}.get((q, s))
                    if t == 0 and c is not None:
                        for tile in range(T):
                            turn_x(0, 1, tile, (c,))
                    if q == 0 and s == 0:
                        pe.wait_ge(xT_lo_ready, parted(0, t, 0))
                    if q == 3 and s == 0 and t == 0:
                        pe.wait_ge(consts_set, 2)
                        pe.wait_ge(rs_diag_ready, T)
                        mm(acc[:, 4, 0:SEQ], ones[:], tok[:, 0:SEQ], start=True, stop=True).then_inc(rs_spread, 1)
                return before

            pe.wait_ge(ident_landed, 16)
            turn_x(0, 1, 0, (0,))
            turn_x(0, 1, 1, (0,))
            for c in range(4):
                if c:
                    pe.wait_ge(xT_lo_ready, parted(0, 1, c))
                quad(Q_V + c, xT_hi, xT_lo, 4 * c, 0, start=c == 0, stop=in0_ready if c == 3 else None,
                     before=turn_next(c))
            pe.wait_ge(rs_row_ready, 1)
            for c in range(4):
                quad(Q_A + c, xT_hi, xT_lo, 4 * c, 1, start=c == 0, stop=in0_ready if c == 3 else None)
                if c == 2:
                    for k in range(8):
                        h = k // 2
                        for t in range(T):
                            pe.wait_ge(v_lo_ready, t + 1)
                            out = acc[:, h, (k % 2) * SEQ + t * P:(k % 2) * SEQ + (t + 1) * P]
                            vs = slice(t * DA + k * P, t * DA + (k + 1) * P)
                            ws = slice(BANK + h * P, BANK + (h + 1) * P)
                            mm(out, vd_hi[:, vs], c_hi[:, 3, ws], start=True, stop=False)
                            mm(out, vd_hi[:, vs], c_lo[:, 3, ws], start=False, stop=False)
                            last = mm(out, vd_lo[:, vs], c_hi[:, 3, ws], start=False, stop=True)
                        if k % 2:
                            last.then_inc(mixed_ready, 1)
            pe.wait_ge(mixed_kept, HEADS)
            for c in range(4):
                for s in range(4):
                    wait_split(Q_U + c, s)
                    for k in range(8):
                        last = block_by_channel(s, k * P, 4 * c + s, k // 2, k % 2, c == 0 and s == 0, c == 3 and s == 3)
                    last.then_inc(units_used, 1)
                if c == 0:
                    pe.wait_ge(a_lo_ready, 4)
                    for k in range(8):
                        g = k // 2
                        out = acc[:, 4 + g, (k % 2) * SEQ:(k % 2 + 1) * SEQ]
                        for t in range(T):
                            a = 8 + 4 * t + k // 2
                            ac = slice((k % 2) * P, (k % 2 + 1) * P)
                            band = (2, slice(g * SEQ, (g + 1) * SEQ)) if t == 0 else (3, slice(g * P, (g + 1) * P))
                            o = out if t == 0 else out[:, P:SEQ]
                            mm(o, mix_hi[:, a, ac], c_hi[:, band[0], band[1]], start=t == 0, stop=False, skip_group_check=True)
                            mm(o, mix_hi[:, a, ac], c_lo[:, band[0], band[1]], start=False, stop=False, skip_group_check=True)
                            last = mm(o, mix_lo[:, a, ac], c_hi[:, band[0], band[1]], start=False, stop=t == 1,
                                      skip_group_check=True)
                        if k % 2:
                            last.then_inc(pooled_ready, 1)
                if c == 1:
                    for g in range(4):
                        pe.wait_ge(pd_lo_ready, g + 1)
                        for n in range(2):
                            out = acc[:, 4 + g, n * SEQ:(n + 1) * SEQ]
                            for cb in range(2):
                                w0 = (g % 2) * 2 * SEQ + cb * SEQ + n * P
                                ws = slice(w0, w0 + P)
                                ds = slice((2 * g + cb) * SEQ, (2 * g + cb + 1) * SEQ)
                                mm(out, c_hi[:, g // 2, ws], vd_hi[:, ds], start=cb == 0, stop=False)
                                mm(out, c_hi[:, g // 2, ws], vd_lo[:, ds], start=False, stop=False)
                                last = mm(out, c_lo[:, g // 2, ws], vd_hi[:, ds], start=False, stop=cb == 1)
                        last.then_inc(group_ready, 1)
            pe.wait_ge(ga_lo_ready, 4)
            for j in range(2):
                for c in range(4):
                    if j == 0 and c >= 2:
                        pe.wait_ge(gb_lo_ready, 2 * c - 2)
                    end = j == 1 and c == 3
                    quad(Q_OUT + 4 * j + c, mix_hi, mix_lo, 4 * c, 1 - j, start=c == 0, stop=y0_ready if c == 3 else None,
                         before=turn_first(1, 0) if end else None, by_tile=end)

            def ffn(layer, q0, b, y_par, par):
                pool = layer == 1
                open_ffn(q0, b, y_par, par, pool)
                x_quads(q0, b, y_par, par, gu0_ready, pool)

                def turn_hidden(i, bank_par):
                    for t in range(T):
                        pe.wait_ge(hid_ready, i * 2 + (22 * layer + t + 1))
                        for n in range(4):
                            last = nc.tensor.transpose(pairs(4 * bank_par + 2 * t)[:, n, :],
                                                       tok[:, t * DA + n * P:t * DA + (n + 1) * P], ident[:])
                        last.then_inc(hid_turned, 1)

                def chunk(i, bank_par):
                    for c in range(4):
                        quad(i * 4 + (q0 + c), xT_hi, xT_lo, 4 * c, bank_par, start=c == 0,
                             stop=gu0_ready if c == 3 else None, after_pool=pool)
                        if c == 0:
                            turn_hidden(i - 1, 1 - bank_par)

                with pe.Fori(0, (FFC - 1) // 2) as n:
                    chunk(n * 2 + 1, 1 - par)
                    chunk(n * 2 + 2, par)
                qd = q0 + Q_FF
                pe.wait_ge(hT_lo_ready, 22 * layer + 20)
                for j in range(2):
                    for c in range(FFC):
                        if j == 0:
                            pe.wait_ge(hT_lo_ready, 22 * layer + 2 * (c + 1))
                        quad(qd + j * FFC + c, hT_hi, hT_lo, 4 * c, par if j else 1 - par, start=c == 0,
                             stop=y0_ready if c == FFC - 1 else None, after_pool=pool, by_tile=j == 1 and c == FFC - 1)
                        if j == 0 and c == 0:
                            turn_hidden(FFC - 1, par)

            ffn(0, Q_F0, 1, 0, 1)

            for t in range(T):
                turn_x(2, 1, t, range(4))

            def add_bias(j):
                for t in range(T):
                    for h in range(2):
                        mm(acc[:, 4 * j + 2 * t + h, :], ones_r[:], bias_rows[:, j * UNIT + h * BANK:j * UNIT + (h + 1) * BANK],
                           start=True, stop=False)

            def conv_in(c, par, dynamic=True):
                for u in range(8):
                    s = u % 4
                    q = c * 2 + (Q_PW1 + u // 4)
                    pe.wait_ge(lo_ready_pool, lo_pool_count(q, s))
                    if not dynamic and c == 0 and u % 2 == 0:
                        pe.wait_ge(xT_lo_ready, parted(2, 1, u // 2))
                    for kk in range(2):
                        k = 2 * u + kk
                        for n in range(4):
                            last = block_by_channel(s, kk * 2 * CC + n * P, k, 4 * par + n % 2, n // 2, k == 0, k == KT - 1)
                    last.then_inc(units_used, 1)

            conv_in(0, 0, False)
            conv_in(1, 1, False)
            with pe.Fori(1, CCH // 2) as i:
                pe.wait_ge(gate_ready, i * 2 - 1)
                conv_in(i * 2, 0)
                pe.wait_ge(gate_ready, i * 2)
                conv_in(i * 2 + 1, 1)

            pe.wait_ge(bias_lo_ready, 1)
            pe.wait_ge(gate_ready, CCH - 1)
            add_bias(0)
            pe.wait_ge(gate_ready, CCH)
            for i in range(2 * TAPS):
                pe.wait_ge(prod_ready, i + 1)
                mm(acc[:, 4, (i % 2) * SEQ:(i % 2 + 1) * SEQ], ident[:], prod[:, i % 4, :], start=i == 0,
                   stop=i >= 2 * TAPS - 2, skip_group_check=True).then_inc(prod_used, 1)

            def sum_channels(n, values, squares, ready, squares_ready):
                for square in range(2):
                    pe.wait_ge(*(squares_ready if square else ready))
                    for b in range(2):
                        src = squares[:, b, :] if square else values[:, b, :]
                        for t in range(T):
                            last = mm(acc[:, 6, 2 * t + square:2 * t + square + 1], src[:, t * P:(t + 1) * P], one_mean[:],
                                      start=n + square + b + t == 0, stop=n == 2 and b == 1, skip_group_check=True)
                last.then_inc(sq_summed, 1)

            pe.wait_ge(consts_set, 5)
            by_pool = (sq_added, 2 * (SQ_POOL - 1))
            sum_channels(0, conv_sum, sq_sum, by_pool, by_pool)
            for n in (1, 2):
                place = SQ_POOL - 1 + n
                c = SQ_ORDER[place]
                sum_channels(n, conv[:, 2 * c:2 * c + 2, :], sq[:, place % 2],
                             (conv_last_ready, 2) if c == CCH - 1 else (conv_ready, 2 * (c + 1)), (sq_ready, place + 1))
            for i in range(2):
                pe.wait_ge(cst_diag_ready, i + 1)
                mm(acc[:, 7 - i, 0:SEQ], ones[:], diag[:, i, :], start=True, stop=True).then_inc(cst_spread, 1)
            for j in range(2):
                if j:
                    add_bias(1)
                for c in range(4):
                    end = j == 1 and c == 3
                    ready = (lambda t, s: pe.wait_ge(cT_lo_ready, 4 * c + s + 1)) if j == 0 else None
                    quad(Q_PW2 + 4 * j + c, cT_hi, cT_lo, 4 * c, j, stop=y0_ready if c == 3 else None,
                         before=turn_first(3, 1) if end else ready, by_tile=end)
            ffn(1, Q_F1, 3, 1, 0)


def bands():
    out = np.zeros((P, 4 * SEQ + 4 * P), np.float32)
    s, t = np.arange(SEQ)[:, None], np.arange(SEQ)[None, :]
    for g, w in enumerate(WINDOWS):
        m = np.where((t >= s) & (t - s < w), np.float32(1) / np.minimum(t + 1, w).astype(np.float32), np.float32(0))
        m = m.astype(np.float32) - (s == t).astype(np.float32)
        out[:, g * SEQ:(g + 1) * SEQ] = m[:P]
        out[:, 4 * SEQ + g * P:4 * SEQ + (g + 1) * P] = m[P:, P:]
    return out


def by_k(w, cols):
    k, n = w.shape
    return w.reshape(k // P, P, n // cols, cols).transpose(2, 0, 1, 3)


def weight_units(ab_w_in, a_w_group, b_w_s, ab_w_out, c_w_pw1, c_w_pw2, f_w_gate, f_w_up, f_w_down):
    band = bands()
    groups = a_w_group[0].reshape(4, 2, P, 2 * P).transpose(2, 0, 1, 3).reshape(P, 2, UNIT).transpose(1, 0, 2)
    spatial = b_w_s[0].transpose(2, 0, 1).reshape(P, HEADS * P)
    w_in = by_k(ab_w_in[0], UNIT)
    out = [w_in[2], groups, band[None, :, :UNIT], np.concatenate([band[:, UNIT:], spatial], axis=1)[None],
           w_in[0], w_in[1]]

    def ffn(i):
        gate_up = np.concatenate([by_k(f_w_gate[i], BANK), by_k(f_w_up[i], BANK)], axis=3)
        return [gate_up.reshape(-1, P, UNIT), by_k(f_w_down[i], UNIT).reshape(-1, P, UNIT)]

    out += [by_k(ab_w_out[0], UNIT).reshape(-1, P, UNIT)] + ffn(0)
    pw1 = c_w_pw1[0].reshape(KT // 2, 2, P, 2, CCH, CC).transpose(4, 0, 2, 1, 3, 5)
    out += [pw1.reshape(-1, P, UNIT), by_k(c_w_pw2[0], UNIT).reshape(-1, P, UNIT)] + ffn(1)
    return np.concatenate([np.asarray(a, np.float32).reshape(-1, P, UNIT) for a in out])


def columns(v):
    return v.reshape(-1, P).T


def kernel(x, ab_norm_pre, ab_w_in, a_w_group, a_scale, b_ln_g, b_ln_b, b_w_s, b_b_s, ab_w_out, ab_norm_post,
           c_norm_pre, c_w_pw1, c_b_pw1, c_w_dw, c_b_dw, c_ln_g, c_ln_b, c_w_pw2, c_b_pw2, c_norm_post,
           f_norm_pre, f_w_gate, f_w_up, f_w_down, f_norm_post):
    import concourse.bacc as bacc
    from concourse.bass_utils import run_bass_kernel_spmd

    a = [np.asarray(v) for v in (ab_w_in, a_w_group, b_w_s, ab_w_out, c_w_pw1, c_w_pw2, f_w_gate, f_w_up, f_w_down)]
    vecs = [ab_norm_pre[0], f_norm_pre[0], c_norm_pre[0], f_norm_pre[1], a_scale[0], c_b_pw1[0], c_b_dw[0],
            c_ln_g[0], c_ln_b[0]]
    arrays = {
        "x": np.asarray(x)[0],
        "units": weight_units(*a),
        "vecs": np.concatenate([columns(np.asarray(v)) for v in vecs], axis=1),
        "taps": np.asarray(c_w_dw)[0].reshape(TAPS, KT, P).transpose(2, 1, 0),
        "ident": np.eye(P, dtype=np.float32),
        "bs": np.asarray(b_b_s),
        "lng": np.asarray(b_ln_g),
        "lnb": np.asarray(b_ln_b),
        "bpw2": np.asarray(c_b_pw2),
        "post": np.stack([np.asarray(v) for v in (ab_norm_post[0], f_norm_post[0], c_norm_post[0], f_norm_post[1])]),
    }
    arrays = {n: np.ascontiguousarray(v) for n, v in arrays.items()}
    nc = bacc.Bacc("TRN2", target_bir_lowering=False, num_devices=1)
    args = [nc.dram_tensor("in_" + n, v.shape, mybir.dt.from_np(v.dtype), kind="ExternalInput").ap() for n, v in arrays.items()]
    out = nc.dram_tensor("out", (SEQ, D), F32, kind="ExternalOutput").ap()
    trunk(nc, *args, out)
    r = run_bass_kernel_spmd(nc, [{"in_" + n: v for n, v in arrays.items()}], core_ids=[0])
    return r.results[0]["out"].reshape(1, SEQ, D)
```
